# Optimizing a Trainium2 kernel written in Bass

```python
import math
import jax
import jax.numpy as jnp
from jax import lax
import numpy as np

D_MODEL = 1024
BATCH = 1
SEQ = 256
DEPTH = 4

GRID_W = 64
CTX_LEN = 256
N_MIXERS = 3
N_A = (DEPTH + 2) // 3
N_B = (DEPTH + 1) // 3
N_C = DEPTH // 3

D_FF = 2816
FFN_CONV = 3

A_HEADS = 16
A_KV_HEADS = 4
A_HEAD_DIM = 64
A_WINDOW = 128
A_BLOCK = 128
ROPE_BASE = 10000.0

B_HEADS = 8
B_HEAD_DIM = 128
B_CONV = 3
B_CHUNK = 64

C_HEADS = 4
C_KEY_DIM = 128
C_VAL_DIM = 256
C_GATE_RANK = 16
C_GATE_TAU = 16.0
C_CHUNK = 64

NORM_EPS = 1e-5
DN_ALPHA = (2 * DEPTH) ** 0.25
DN_BETA = (8 * DEPTH) ** -0.25

kernel_name = 'hybrid_interleaved_swa_gdn_gla_prefix_dit'

def layer_norm(t, g, b):
    tf = t.astype(jnp.float32)
    mu = jnp.mean(tf, -1, keepdims=True)
    var = jnp.mean(jnp.square(tf - mu), -1, keepdims=True)
    return ((tf - mu) * lax.rsqrt(var + NORM_EPS)).astype(t.dtype) * g + b

def rms_norm(t, g):
    tf = t.astype(jnp.float32)
    return (tf * lax.rsqrt(jnp.mean(tf * tf, -1, keepdims=True) + NORM_EPS)).astype(t.dtype) * g

def l2_normalize(t):
    return t * lax.rsqrt(jnp.sum(t * t, -1, keepdims=True) + 1e-6)

def modulate(t, shift, scale):
    return t * (1 + scale) + shift

def dwconv(t, w):
    k = w.shape[0]
    pad = (k - 1) // 2
    return lax.conv_general_dilated(t, w[:, None, :].astype(t.dtype), window_strides=(1,),
                                    padding=[(pad, pad)], dimension_numbers=('NWC', 'WIO', 'NWC'),
                                    feature_group_count=t.shape[-1])

def axial_rope(rows):
    r = jnp.repeat(jnp.arange(rows), GRID_W).astype(jnp.float32)
    col = jnp.tile(jnp.arange(GRID_W), rows).astype(jnp.float32)
    n_freq = A_HEAD_DIM // 4
    inv = jnp.power(ROPE_BASE, -jnp.arange(n_freq, dtype=jnp.float32) / n_freq)
    ang = jnp.concatenate([r[:, None] * inv, col[:, None] * inv], -1)
    return jnp.cos(ang), jnp.sin(ang)

def apply_rope(t, cos, sin):
    half = t.shape[-1] // 2
    shape = (cos.shape[0],) + (1,) * (t.ndim - 3) + (half,)
    cs = cos.reshape(shape).astype(t.dtype)
    sn = sin.reshape(shape).astype(t.dtype)
    t1, t2 = t[..., :half], t[..., half:]
    return jnp.concatenate([t1 * cs - t2 * sn, t1 * sn + t2 * cs], -1)

def window_attention(u, uc, w_qkv, sink, w_o, cos, sin, need_ctx_out):
    bsz, n, _ = u.shape
    n_ctx = uc.shape[1]
    grp = A_HEADS // A_KV_HEADS
    nq = A_HEADS * A_HEAD_DIM
    nkv = A_KV_HEADS * A_HEAD_DIM
    scale = A_HEAD_DIM ** -0.5
    span = A_BLOCK + 2 * A_WINDOW

    def heads_q(t):
        return t.reshape(t.shape[0], t.shape[1], A_KV_HEADS, grp, A_HEAD_DIM)

    def heads_kv(t):
        return t.reshape(t.shape[0], t.shape[1], A_KV_HEADS, A_HEAD_DIM)

    qkv = u @ w_qkv
    q = apply_rope(heads_q(qkv[..., :nq]), cos, sin) * scale
    k = apply_rope(heads_kv(qkv[..., nq:nq + nkv]), cos, sin)
    v = heads_kv(qkv[..., nq + nkv:])
    kvc = uc @ w_qkv[:, nq:]
    kc = heads_kv(kvc[..., :nkv])
    vc = heads_kv(kvc[..., nkv:])
    sink_l = sink.reshape(A_KV_HEADS, grp).astype(jnp.float32)

    kp = jnp.pad(k, ((0, 0), (A_WINDOW, A_WINDOW), (0, 0), (0, 0)))
    vp = jnp.pad(v, ((0, 0), (A_WINDOW, A_WINDOW), (0, 0), (0, 0)))
    rel = jnp.arange(span)[None, :] - jnp.arange(A_BLOCK)[:, None]
    band = (rel >= 0) & (rel <= 2 * A_WINDOW)

    def block(bi):
        start = bi * A_BLOCK
        qb = lax.dynamic_slice_in_dim(q, start, A_BLOCK, axis=1)
        kb = lax.dynamic_slice_in_dim(kp, start, span, axis=1)
        vb = lax.dynamic_slice_in_dim(vp, start, span, axis=1)
        kpos = start - A_WINDOW + jnp.arange(span)
        valid = band & ((kpos >= 0) & (kpos < n))[None, :]
        s_loc = jnp.where(valid, jnp.einsum('bqkgd,bskd->bkgqs', qb, kb).astype(jnp.float32), -jnp.inf)
        s_ctx = jnp.einsum('bqkgd,bskd->bkgqs', qb, kc).astype(jnp.float32)
        s_snk = jnp.broadcast_to(sink_l[None, :, :, None, None], s_ctx.shape[:-1] + (1,))
        p = jax.nn.softmax(jnp.concatenate([s_loc, s_ctx, s_snk], -1), axis=-1).astype(u.dtype)
        return (jnp.einsum('bkgqs,bskd->bqkgd', p[..., :span], vb)
                + jnp.einsum('bkgqs,bskd->bqkgd', p[..., span:span + n_ctx], vc))

    o = lax.map(block, jnp.arange(n // A_BLOCK))
    y = jnp.moveaxis(o, 0, 1).reshape(bsz, n, nq) @ w_o
    yc = None
    if need_ctx_out:
        qc = heads_q(uc @ w_qkv[:, :nq]) * scale
        s = jnp.einsum('bqkgd,bskd->bkgqs', qc, kc).astype(jnp.float32)
        s_snk = jnp.broadcast_to(sink_l[None, :, :, None, None], s.shape[:-1] + (1,))
        p = jax.nn.softmax(jnp.concatenate([s, s_snk], -1), axis=-1).astype(uc.dtype)
        oc = jnp.einsum('bkgqs,bskd->bqkgd', p[..., :n_ctx], vc)
        yc = oc.reshape(bsz, n_ctx, nq) @ w_o
    return y, yc

def gated_delta_chunk_scan(q, k, v, beta, g, state):
    bsz, h, n, dk = q.shape
    dv = v.shape[-1]
    nc = n // B_CHUNK

    def chunk(t):
        return t.reshape((bsz, h, nc, B_CHUNK) + t.shape[3:])

    q, k, v, beta, g = chunk(q), chunk(k), chunk(v), chunk(beta), chunk(g)
    gc = jnp.cumsum(g, axis=-1)
    tri = jnp.tril(jnp.ones((B_CHUNK, B_CHUNK), bool))
    strict = jnp.tril(jnp.ones((B_CHUNK, B_CHUNK), bool), -1)
    decay = jnp.where(tri, jnp.exp(jnp.where(tri, gc[..., :, None] - gc[..., None, :], 0.0)), 0.0)
    kb = k * beta[..., None]
    lmat = jnp.where(strict, jnp.einsum('bhncd,bhnsd->bhncs', kb, k) * decay, 0.0)
    eye = jnp.eye(B_CHUNK, dtype=q.dtype)
    tmat = lax.linalg.triangular_solve(eye + lmat, jnp.broadcast_to(eye, lmat.shape), left_side=True, lower=True)
    u_w = tmat @ (v * beta[..., None])
    w_w = tmat @ (kb * jnp.exp(gc)[..., None])
    a_qk = jnp.einsum('bhncd,bhnsd->bhncs', q, k) * decay
    q_dec = q * jnp.exp(gc)[..., None]
    g_last = gc[..., -1]
    k_dec = k * jnp.exp(g_last[..., None] - gc)[..., None]
    xs = tuple(jnp.moveaxis(t, 2, 0) for t in (q_dec, k_dec, u_w, w_w, a_qk, g_last))

    def step(s, inp):
        qd, kd, uu, ww, aa, gl = inp
        v_new = uu - ww @ s
        o = qd @ s + aa @ v_new
        s = s * jnp.exp(gl)[..., None, None] + jnp.einsum('bhcd,bhce->bhde', kd, v_new)
        return s, o

    state, o = lax.scan(step, state, xs)
    return jnp.moveaxis(o, 0, 2).reshape(bsz, h, n, dv), state

def gla_chunk_scan(q, k, v, log_a, state):
    bsz, h, n, dk = q.shape
    dv = v.shape[-1]
    nc = n // C_CHUNK

    def chunk(t):
        return jnp.moveaxis(t.reshape(bsz, h, nc, C_CHUNK, t.shape[-1]), 2, 0)

    q, k, v, la = chunk(q), chunk(k), chunk(v), chunk(log_a)
    bcum = jnp.cumsum(la, axis=-2)
    tri = jnp.tril(jnp.ones((C_CHUNK, C_CHUNK), bool))[:, :, None]

    def step(s, inp):
        qi, ki, vi, bi = inp
        rel = jnp.exp(jnp.where(tri, bi[:, :, :, None, :] - bi[:, :, None, :, :], -jnp.inf))
        a = jnp.einsum('bhid,bhjd,bhijd->bhij', qi, ki, rel)
        bl = bi[:, :, -1:, :]
        o = (qi * jnp.exp(bi)) @ s + a @ vi
        s = jnp.exp(bl)[:, :, 0, :, None] * s + jnp.einsum('bhjd,bhje->bhde', ki * jnp.exp(bl - bi), vi)
        return s, o

    state, o = lax.scan(step, state, (q, k, v, bcum))
    return jnp.moveaxis(o, 0, 2).reshape(bsz, h, n, dv), state

def bidirectional_scan(scan_fn, fwd_args, bwd_args, s_fwd, s_bwd):
    o_f, st_f = scan_fn(*fwd_args, s_fwd)
    o_b, st_b = scan_fn(*[jnp.flip(t, 2) for t in bwd_args], s_bwd)
    return o_f + jnp.flip(o_b, 2), st_f, st_b

def gated_deltanet(u, uc, w_in, conv_w, a_log, dt_bias, norm_w, w_o, need_ctx_out):
    hk = B_HEADS * B_HEAD_DIM

    def prep(t):
        bsz, n, _ = t.shape
        z = t @ w_in
        qkv = jax.nn.silu(dwconv(z[..., :3 * hk], conv_w)).astype(jnp.float32)

        def heads(a):
            return a.reshape(bsz, n, B_HEADS, B_HEAD_DIM).transpose(0, 2, 1, 3)

        q = l2_normalize(heads(qkv[..., :hk])) * (B_HEAD_DIM ** -0.5)
        k = l2_normalize(heads(qkv[..., hk:2 * hk]))
        v = heads(qkv[..., 2 * hk:])
        gate = z[..., 3 * hk:4 * hk]
        b_raw = z[..., 4 * hk:4 * hk + 2 * B_HEADS].astype(jnp.float32).reshape(bsz, n, 2, B_HEADS)
        a_raw = z[..., 4 * hk + 2 * B_HEADS:].astype(jnp.float32).reshape(bsz, n, 2, B_HEADS)
        beta = jax.nn.sigmoid(b_raw).transpose(2, 0, 3, 1)
        g = (-jnp.exp(a_log.astype(jnp.float32)) * jax.nn.softplus(a_raw + dt_bias.astype(jnp.float32))).transpose(2, 0, 3, 1)
        return q, k, v, beta, g, gate

    def finish(o, gate):
        bsz, _, n, _ = o.shape
        o = rms_norm(o.transpose(0, 2, 1, 3), norm_w.astype(jnp.float32)).astype(gate.dtype)
        o = o * jax.nn.silu(gate.reshape(bsz, n, B_HEADS, B_HEAD_DIM))
        return o.reshape(bsz, n, hk) @ w_o

    qc, kc, vc, betac, gcx, gatec = prep(uc)
    zero = jnp.zeros((uc.shape[0], B_HEADS, B_HEAD_DIM, B_HEAD_DIM), jnp.float32)
    oc, s_f, s_b = bidirectional_scan(gated_delta_chunk_scan, (qc, kc, vc, betac[0], gcx[0]),
                                      (qc, kc, vc, betac[1], gcx[1]), zero, zero)
    q, k, v, beta, g, gate = prep(u)
    o, _, _ = bidirectional_scan(gated_delta_chunk_scan, (q, k, v, beta[0], g[0]),
                                 (q, k, v, beta[1], g[1]), s_f, s_b)
    y = finish(o, gate)
    yc = finish(oc, gatec) if need_ctx_out else None
    return y, yc

def gla_mixer(u, uc, w_in, w_gate2, gate_b, norm_w, w_o, need_ctx_out):
    dk_all = C_HEADS * C_KEY_DIM
    dv_all = C_HEADS * C_VAL_DIM

    def prep(t):
        bsz, n, _ = t.shape
        z = t @ w_in
        f = z.astype(jnp.float32)

        def heads(a, dim):
            return a.reshape(bsz, n, C_HEADS, dim).transpose(0, 2, 1, 3)

        q = heads(f[..., :dk_all], C_KEY_DIM) * (C_KEY_DIM ** -0.5)
        k = heads(f[..., dk_all:2 * dk_all], C_KEY_DIM)
        v = heads(f[..., 2 * dk_all:2 * dk_all + dv_all], C_VAL_DIM)
        gate = z[..., 2 * dk_all + dv_all:2 * dk_all + 2 * dv_all]
        low = f[..., 2 * dk_all + 2 * dv_all:].reshape(bsz, n, 2, C_GATE_RANK)
        logit = jnp.einsum('blzr,zrd->zbld', low, w_gate2.astype(jnp.float32)) + gate_b.astype(jnp.float32)[:, None, None, :]
        log_a = (jax.nn.log_sigmoid(logit) / C_GATE_TAU).reshape(2, bsz, n, C_HEADS, C_KEY_DIM).transpose(0, 1, 3, 2, 4)
        return q, k, v, log_a, gate

    def finish(o, gate):
        bsz, _, n, _ = o.shape
        o = rms_norm(o.transpose(0, 2, 1, 3), norm_w.astype(jnp.float32)).astype(gate.dtype)
        o = o * jax.nn.silu(gate.reshape(bsz, n, C_HEADS, C_VAL_DIM))
        return o.reshape(bsz, n, dv_all) @ w_o

    qc, kc, vc, lac, gatec = prep(uc)
    zero = jnp.zeros((uc.shape[0], C_HEADS, C_KEY_DIM, C_VAL_DIM), jnp.float32)
    oc, s_f, s_b = bidirectional_scan(gla_chunk_scan, (qc, kc, vc, lac[0]), (qc, kc, vc, lac[1]), zero, zero)
    q, k, v, la, gate = prep(u)
    o, _, _ = bidirectional_scan(gla_chunk_scan, (q, k, v, la[0]), (q, k, v, la[1]), s_f, s_b)
    y = finish(o, gate)
    yc = finish(oc, gatec) if need_ctx_out else None
    return y, yc

def conv_glu(t, w_up, conv_w, conv_b, w_down):
    hdn = t @ w_up
    val, gt = hdn[..., :D_FF], hdn[..., D_FF:]
    gt = dwconv(gt, conv_w) + conv_b
    return (jax.nn.silu(gt) * val) @ w_down

def setup_inputs(seed: int = 0) -> dict:
    key = jax.random.key(seed)
    ks = iter(jax.random.split(key, 32))

    def nrm(shape, scale):
        return jax.random.normal(next(ks), shape, jnp.float32) * scale

    d = D_MODEL
    a_qkv = (A_HEADS + 2 * A_KV_HEADS) * A_HEAD_DIM
    a_out = A_HEADS * A_HEAD_DIM
    b_w = B_HEADS * B_HEAD_DIM
    b_in = 4 * b_w + 4 * B_HEADS
    c_k = C_HEADS * C_KEY_DIM
    c_v = C_HEADS * C_VAL_DIM
    c_in = 2 * c_k + 2 * c_v + 2 * C_GATE_RANK
    x = nrm((BATCH, SEQ, d), 1.0)
    c = nrm((BATCH, d), 1.0)
    ctx = nrm((BATCH, CTX_LEN, d), 1.0)
    c_ctx = nrm((d,), 1.0)
    ada_w = nrm((DEPTH, d, 6 * d), d ** -0.5)
    ada_b = nrm((DEPTH, 6 * d), 0.02)
    ln_g = 1.0 + nrm((DEPTH, 2, d), 0.02)
    ln_b = nrm((DEPTH, 2, d), 0.02)
    ffn_w_up = nrm((DEPTH, d, 2 * D_FF), d ** -0.5)
    ffn_conv_w = nrm((DEPTH, FFN_CONV, D_FF), FFN_CONV ** -0.5)
    ffn_conv_b = nrm((DEPTH, D_FF), 0.02)
    ffn_w_down = nrm((DEPTH, D_FF, d), DN_BETA * D_FF ** -0.5)
    attn_w_qkv = nrm((N_A, d, a_qkv), d ** -0.5)
    attn_sink = nrm((N_A, A_HEADS), 0.5)
    attn_w_o = nrm((N_A, a_out, d), DN_BETA * a_out ** -0.5)
    gdn_w_in = nrm((N_B, d, b_in), d ** -0.5)
    gdn_conv_w = nrm((N_B, B_CONV, 3 * b_w), B_CONV ** -0.5)
    gdn_a_log = jnp.log(jax.random.uniform(next(ks), (N_B, 2, B_HEADS), jnp.float32, 1.0, 16.0))
    dt = jnp.exp(jax.random.uniform(next(ks), (N_B, 2, B_HEADS), jnp.float32, math.log(1e-3), math.log(1e-1)))
    gdn_dt_bias = dt + jnp.log(-jnp.expm1(-dt))
    gdn_norm_w = 1.0 + nrm((N_B, B_HEAD_DIM), 0.02)
    gdn_w_o = nrm((N_B, b_w, d), DN_BETA * b_w ** -0.5)
    gla_w_in = nrm((N_C, d, c_in), d ** -0.5)
    gla_w_gate2 = nrm((N_C, 2, C_GATE_RANK, c_k), C_GATE_RANK ** -0.5)
    gla_gate_b = nrm((N_C, 2, c_k), 0.02)
    gla_norm_w = 1.0 + nrm((N_C, C_VAL_DIM), 0.02)
    gla_w_o = nrm((N_C, c_v, d), DN_BETA * c_v ** -0.5)
    return {'x': x, 'c': c, 'ctx': ctx, 'c_ctx': c_ctx, 'ada_w': ada_w, 'ada_b': ada_b,
            'ln_g': ln_g, 'ln_b': ln_b, 'ffn_w_up': ffn_w_up, 'ffn_conv_w': ffn_conv_w,
            'ffn_conv_b': ffn_conv_b, 'ffn_w_down': ffn_w_down, 'attn_w_qkv': attn_w_qkv,
            'attn_sink': attn_sink, 'attn_w_o': attn_w_o, 'gdn_w_in': gdn_w_in, 'gdn_conv_w': gdn_conv_w,
            'gdn_a_log': gdn_a_log, 'gdn_dt_bias': gdn_dt_bias, 'gdn_norm_w': gdn_norm_w, 'gdn_w_o': gdn_w_o,
            'gla_w_in': gla_w_in, 'gla_w_gate2': gla_w_gate2, 'gla_gate_b': gla_gate_b,
            'gla_norm_w': gla_norm_w, 'gla_w_o': gla_w_o}

def reference(x, c, ctx, c_ctx, ada_w, ada_b, ln_g, ln_b, ffn_w_up, ffn_conv_w, ffn_conv_b, ffn_w_down,
              attn_w_qkv, attn_sink, attn_w_o, gdn_w_in, gdn_conv_w, gdn_a_log, gdn_dt_bias, gdn_norm_w, gdn_w_o,
              gla_w_in, gla_w_gate2, gla_gate_b, gla_norm_w, gla_w_o):
    bsz, n, d = x.shape
    rows = n // GRID_W
    cos, sin = axial_rope(rows)
    xc = ctx
    s_lat = jax.nn.silu(c)
    s_ctx = jax.nn.silu(c_ctx)
    for i in range(DEPTH):
        need_ctx_out = i < DEPTH - 1
        mod = (s_lat @ ada_w[i] + ada_b[i]).reshape(bsz, 6, 1, d)
        modc = (s_ctx @ ada_w[i] + ada_b[i]).reshape(6, 1, d)
        u = modulate(x, mod[:, 0], mod[:, 1])
        uc = modulate(xc, modc[0], modc[1])
        kind, slot = i % N_MIXERS, i // N_MIXERS
        if kind == 0:
            y, yc = window_attention(u, uc, attn_w_qkv[slot], attn_sink[slot], attn_w_o[slot], cos, sin, need_ctx_out)
        elif kind == 1:
            y, yc = gated_deltanet(u, uc, gdn_w_in[slot], gdn_conv_w[slot], gdn_a_log[slot], gdn_dt_bias[slot],
                                   gdn_norm_w[slot], gdn_w_o[slot], need_ctx_out)
        else:
            y, yc = gla_mixer(u, uc, gla_w_in[slot], gla_w_gate2[slot], gla_gate_b[slot], gla_norm_w[slot],
                              gla_w_o[slot], need_ctx_out)
        x = layer_norm(DN_ALPHA * x + mod[:, 2] * y, ln_g[i, 0], ln_b[i, 0])
        h = modulate(x, mod[:, 3], mod[:, 4])
        x = layer_norm(DN_ALPHA * x + mod[:, 5] * conv_glu(h, ffn_w_up[i], ffn_conv_w[i], ffn_conv_b[i], ffn_w_down[i]),
                       ln_g[i, 1], ln_b[i, 1])
        if need_ctx_out:
            xc = layer_norm(DN_ALPHA * xc + modc[2] * yc, ln_g[i, 0], ln_b[i, 0])
            hc = modulate(xc, modc[3], modc[4])
            xc = layer_norm(DN_ALPHA * xc + modc[5] * conv_glu(hc, ffn_w_up[i], ffn_conv_w[i], ffn_conv_b[i], ffn_w_down[i]),
                            ln_g[i, 1], ln_b[i, 1])
    return x


_drawn_inputs = setup_inputs


def setup_inputs(seed=0):
    import zlib

    import numpy as np

    out = dict(_drawn_inputs(seed))
    spreads = {}
    factors = {'ada_b': 2.754,
     'ffn_conv_b': 8.0,
     'attn_sink': 8.0,
     'gdn_a_log': 2.892,
     'gdn_norm_w': 22.932,
     'gla_gate_b': 8.0,
     'gla_norm_w': 28.674}
    for name, (base, spread) in spreads.items():
        noise = np.random.default_rng([zlib.crc32(name.encode()), seed]).standard_normal(out[name].shape)
        drawn = base * np.exp(spread * noise) if base else spread * noise
        out[name] = jnp.asarray(drawn.astype(out[name].dtype))
    for name, factor in factors.items():
        out[name] = (out[name] * factor).astype(out[name].dtype)
    return out
```

```python
from contextlib import ExitStack, contextmanager

import numpy as np

import concourse.bass as bass
from concourse import mybir

ALU = mybir.AluOpType
ACT = mybir.ActivationFunctionType
AX = mybir.AxisListType
F32 = mybir.dt.float32
F32R = mybir.dt.float32r
U8 = mybir.dt.uint8

P = 128
D = 1024
KT = D // P
CTX = 256
SEQ = 256
TOK = CTX + SEQ
TT = TOK // P
DEPTH = 4
LAYERS = 4
D_FF = 2816
FT = D_FF // P
EPS = 1e-5
ALPHA = (2 * DEPTH) ** 0.25
MOD = 6 * KT
UNIT = KT * 256
PIECE = UNIT // 4
ADA_UNITS = 6 * D // 256
ADA_FIRST = 2 * D // 256
ADA_SLOTS = 6
NEG = -1e30
A_HEADS, A_KV, A_HD = 16, 4, 64
A_Q = A_HEADS * A_HD
A_SCALE = A_HD ** -0.5
GRID_W = 64
B_HEADS, B_HD = 8, 128
B_TAIL = 4 * B_HEADS
C_HEADS, C_KD, C_VD, C_RANK, C_TAU = 4, 128, 256, 16, 16.0
C_TAIL = 2 * C_RANK
C_K = C_HEADS * C_KD
LEVELS = (1, 2, 4, 8, 16, 32, 64)
NL = len(LEVELS)

ADAB = lambda l, j: (l // 2) * P + (l % 2) * MOD + j
LNG = lambda l, w, t: 2 * P + (l * 2 + w) * KT + t
LNB = lambda l, w, t: 2 * P + 64 + (l * 2 + w) * KT + t
CONVW = lambda l, tap: 3 * P + (l * 3 + tap) * FT
CONVB = lambda l: 3 * P + DEPTH * 3 * FT + l * FT
CVEC = 3 * P + DEPTH * 4 * FT
GDNCW = lambda tap: 6 * P + tap * 24
GDNNW = 6 * P + 72
GLANW = 6 * P + 73
ROWT = 7
ROWS = (96, 96, 128, 128, 128, 112, 75)
STAT = ((4, 5), (0, 1))

K_ID, K_ONE, K_MEAN, K_TRI, K_TRIB, K_STR, K_STRB, K_ROT, K_AM = [P * i for i in range(9)]
K_COS = K_AM + 2 * P
K_SIN = K_COS + SEQ
K_COL = K_SIN + SEQ
K_N = K_COL + 4


def constants():
    i = np.arange(P)
    c = np.zeros((P, K_N), np.float32)
    c[:, K_ID:K_ID + P] = np.eye(P)
    c[:, K_ONE:K_ONE + P] = 1
    c[:, K_MEAN:K_MEAN + P] = 1.0 / D
    c[:, K_TRI:K_TRI + P] = i[:, None] <= i
    c[:, K_TRIB:K_TRIB + P] = i[:, None] >= i
    c[:, K_STR:K_STR + P] = i[:, None] < i
    c[:, K_STRB:K_STRB + P] = i[:, None] > i
    half = A_HD // 2
    for m in range(P):
        if m % A_HD < half:
            c[m + half, K_ROT + m] = -1
        else:
            c[m - half, K_ROT + m] = 1
    c[:, K_AM:K_AM + P] = np.where(i[None, :] > i[:, None], NEG, 0)
    c[:, K_AM + P:K_AM + 2 * P] = np.where(i[None, :] < i[:, None], NEG, 0)
    n_freq = A_HD // 4
    inv = np.power(np.float32(10000.0), -np.arange(n_freq, dtype=np.float32) / np.float32(n_freq))
    t = np.arange(SEQ)
    ang = np.concatenate([(t // GRID_W)[:, None].astype(np.float32) * inv,
                          (t % GRID_W)[:, None].astype(np.float32) * inv], -1).astype(np.float32)
    c[:, K_COS:K_COS + SEQ] = np.cos(ang).T[i % half]
    c[:, K_SIN:K_SIN + SEQ] = np.sin(ang).T[i % half]
    c[:, K_COL] = EPS / ALPHA ** 2
    c[:, K_COL + 1] = 1e-6
    c[:, K_COL + 2] = EPS
    m = np.zeros((P, 2 * NL + 1, P), np.float32)
    for n, b in enumerate(LEVELS):
        up = (i[:, None] // (2 * b) == i // (2 * b)) & (i[:, None] % (2 * b) < b) & (i % (2 * b) >= b)
        m[:, n], m[:, NL + n] = up, up.T
    m[:, 2 * NL] = np.eye(P)
    return c, m.reshape(P, -1)


class Engine:

    def __init__(self, eng, own, gate):
        self.eng, self.own, self.gate = eng, own, gate
        self.at, self.turn = {}, None

    def skip(self, sem, n=1):
        k = sem.name
        self.at[k] = self.at.get(k, 0) + n

    def next(self, sem, n=1):
        self.skip(sem, n)
        v = self.at[sem.name]
        return v if self.turn is None else v + self.turn[0] * self.turn[1][sem.name]

    def step(self):
        self.skip(self.own)
        return 1

    def count(self):
        return self.next(self.own, 0)

    def stand(self):
        if self.turn is not None:
            self.eng.sem_inc(self.gate, 1)

    @contextmanager
    def loop(self, n, per):
        per = {s.name: k for s, k in per.items()}
        before = dict(self.at)
        with self.eng.Fori(0, n) as i:
            self.turn = (i, per)
            yield i
            self.turn = None
        moved = {k: v - before.get(k, 0) for k, v in self.at.items() if v != before.get(k, 0)}
        assert moved == per, (self.own.name, moved, per)
        for k, v in per.items():
            self.at[k] += (n - 1) * v


def build(nc, a, out):
    with ExitStack() as ctx:
        top = [nc.sbuf_base + (-nc.sbuf_base) % 64]

        def sb(name, shape, dt=F32, at=None):
            size = int(np.prod(shape[1:])) * (1 if dt == U8 else 4)
            if at is None:
                at = top[0]
                top[0] += (size + 63) // 64 * 64
            assert at + size <= nc.sbuf_usable_end, (name, at + size)
            return nc.alloc_sbuf_tensor_at(name, shape, dt, offset=at)

        sem = lambda n: ctx.enter_context(nc.semaphore(n))
        bank = [ctx.enter_context(nc.psum_tensor(f"bank{i}", [P, 512], F32)) for i in range(8)]

        con = sb("con", [P, K_N])
        msk = sb("msk", [P, 2 * NL + 1, P], U8)
        vec = sb("vec", [P, ROWT * P])
        mod = sb("mod", [P, DEPTH, MOD, 2])
        aff = sb("aff", [P, DEPTH, 4, KT, 2])
        gat = sb("gat", [P, DEPTH, 2, KT, 2])
        sT = sb("sT", [P, KT, 2])
        x = sb("x", [P, KT, TOK])
        w_raw = sb("w_raw", [P, 2, UNIT])
        w_hi = sb("w_hi", [P, 4, PIECE], F32R)
        w_lo = sb("w_lo", [P, 4, PIECE], F32R)
        U0 = top[0]
        u_hi = sb("u_hi", [P, KT, TOK], F32R)
        u_lo = sb("u_lo", [P, KT, TOK], F32R)
        ADA0 = top[0]
        ada_w = sb("ada_w", [P, 2, UNIT])
        ada_0 = sb("ada_0", [P, ADA_SLOTS, UNIT], at=U0)
        LN0 = top[0]
        sq = sb("sq", [P, 4, TOK])
        u32 = sb("u32", [P, 2, TOK])
        acc = sb("acc", [P, 2, 2, 256], at=LN0 + 4 * 2048)
        rstd = sb("rstd", [P, TOK])
        sink = sb("sink", [P, 2, A_HEADS])
        nsink = sb("nsink", [P, 2, A_HEADS])
        warm = sb("warm", [P, 1])
        gdp = sb("gdp", [P, 2, 2 * B_HEADS])
        tw_hi = sb("tail_hi", [P, KT, B_TAIL], F32R)
        tw_lo = sb("tail_lo", [P, KT, B_TAIL], F32R)
        AR0 = top[0]
        K4 = 2048
        xin = sb("xin", [P, TT, D], at=AR0)
        rows = sb("rows", [P, ROWT, P], at=AR0 + TT * D * 4)
        msk_f = sb("msk_f", [P, 2 * NL + 1, P], at=AR0 + (TT * D + ROWT * P) * 4)
        xout = sb("xout", [P, 2, D], at=AR0)
        g = sb("g", [P, FT, TOK], at=AR0)
        gs_hi = sb("gs_hi", [P, 4, TOK], F32R, at=AR0 + FT * K4)
        gs_lo = sb("gs_lo", [P, 4, TOK], F32R, at=AR0 + (FT + 4) * K4)
        cv = sb("cv", [P, 2, TOK], at=AR0 + (FT + 8) * K4)
        aq = sb("aq", [P, KT, TOK], at=AR0)
        ak = sb("ak", [P, 2, TOK], at=AR0 + 8 * K4)
        akd = sb("akd", [P, A_KV, TOK], at=AR0 + 10 * K4)
        av = sb("av", [P, TT, 256], at=AR0 + 14 * K4)
        ap_ = sb("ap", [P, 4, TOK], at=AR0 + 16 * K4)
        apt = sb("apt", [P, 2, TOK], at=AR0 + 20 * K4)
        art = sb("art", [P, 2, SEQ], at=AR0 + 22 * K4)
        ast = sb("ast", [P, 5, 4], at=AR0 + 23 * K4)

        bq = sb("bq", [P, B_HEADS, TOK], at=AR0)
        bk = sb("bk", [P, B_HEADS, TOK], at=AR0 + 8 * K4)
        bv = sb("bv", [P, TT, B_HEADS, P], at=AR0 + 16 * K4)
        bo = sb("bo", [P, B_HEADS, TOK], at=AR0 + 24 * K4)
        bg = sb("bg", [P, B_HEADS, TOK], at=ADA0)
        bS = sb("bS", [P, 2, B_HEADS, P], at=LN0)
        bc = sb("bc", [P, 2, TOK], at=LN0)
        bsq = sb("bsq", [P, 2, TOK], at=LN0 + 2 * K4)
        brn = sb("brn", [P, 2, TOK], at=LN0 + 4 * K4)
        H2 = 2 * B_HEADS
        B0 = LN0 + 4 * K4
        bsm = [sb(f"bsm{i}", [P, TT, H2], at=B0 + 256 * i) for i in range(11)]
        b_x, b_ax, b_e, b_ln, b_g, b_beta, b_nbeta, b_ngc, b_negc, b_kd, b_egl = bsm
        tw = sb("tail_w", [P, KT, B_TAIL], at=B0 + 256 * 11)
        bt = [[sb(f"b{n}{d}", [P, 4, P], at=U0 + (7 * d + i) * K4) for i, n in enumerate(("D", "E", "AT", "NL", "T", "TT", "A"))]
              for d in range(2)]

        cq = sb("cq", [P, C_HEADS, TOK], at=AR0)
        ck = sb("ck", [P, C_HEADS, TOK], at=AR0 + 4 * K4)
        cvt = sb("cvt", [P, TT, C_HEADS * C_VD], at=AR0 + 8 * K4)
        cla = sb("cla", [P, TT, 2 * C_K], at=AR0 + 16 * K4)
        cAT = sb("cAT", [P, C_HEADS, TOK], at=AR0 + 24 * K4)
        ckl = sb("ckl", [P, C_HEADS, TT, P], at=AR0 + 28 * K4)
        cqe = sb("cqe", [P, C_HEADS, TOK], at=U0)
        cqf = sb("cqf", [P, 2, TOK], at=U0 + 4 * K4)
        ckf = sb("ckf", [P, 2, TOK], at=U0 + 6 * K4)
        co = sb("co", [P, KT, TOK], at=U0 + 8 * K4)
        cg = sb("cg", [P, KT, TOK], at=ADA0)
        cS = sb("cS", [P, C_HEADS, C_VD], at=LN0)
        cF = sb("cF", [P, 2, TOK], at=LN0 + 2 * K4)
        cb = sb("cb", [P, 2, TOK], at=LN0 + 4 * K4)
        clow = sb("clow", [33, TOK], at=LN0)
        cw2 = sb("cw2", [33, 2 * C_K], at=LN0 + K4)
        clg = sb("clg", [P, 3, TOK], at=LN0 + 3 * K4)
        ctw = sb("ctw", [P, KT, C_TAIL], at=LN0 + 6 * K4)
        clt = sb("clt", [P, P], at=LN0 + 6 * K4 + 1024)
        cel = sb("cel", [P, C_HEADS, TT], at=LN0 + 6 * K4 + 1536)

        s_con = sem("constants_loaded")
        s_in = sem("inputs_loaded")
        w_loaded = [sem("unit_loaded_0"), sem("unit_loaded_1")]
        w_split = sem("piece_split")
        w_done = sem("piece_multiplied")
        ada_loaded = [sem("ada_loaded_0"), sem("ada_loaded_1")]
        ada_0_loaded = [sem(f"ada_0_loaded_{i}") for i in range(ADA_SLOTS)]
        ada_summed = sem("ada_products_summed")
        ada_done = sem("ada_multiplied")
        mod_ready = sem("modulation_ready")
        rows_t = sem("rows_transposed")
        vec_ready = sem("vectors_ready")
        st_ready = sem("silu_c_ready")
        xt_done = sem("x_transposed")
        xt_copied = sem("x_copied")
        r_ready = sem("residual_ready")
        mean_ready = sem("mean_ready")
        c_ready = sem("centred_ready")
        sq_ready = sem("square_ready")
        sq_used = sem("square_used")
        var_ready = sem("variance_ready")
        std_ready = sem("deviation_ready")
        xh_ready = sem("normed_ready")
        uhi_ready = sem("u_hi_ready")
        u_ready = sem("u_ready")
        x_ready = sem("x_ready")
        conv_c = sem("conv_centre_ready")
        conv_done = sem("conv_done")
        silu_done = sem("silu_done")
        g_done = sem("gated_done")
        gs_h = sem("g_hi_ready")
        gs_ready = sem("g_split_ready")
        pair_free = sem("pair_read")
        out_stored = sem("out_stored")
        tail_loaded = sem("tail_loaded")
        tail_h = sem("tail_hi_ready")
        tail_ready = sem("tail_ready")
        tail_done = sem("tail_multiplied")
        sq_h = sem("head_squares_ready")
        ss_ready = sem("head_sums_ready")
        rt_ready = sem("head_roots_ready")
        hn_ready = sem("heads_normed")
        hv_ready = sem("values_ready")
        tr_ready = sem("head_transposed")
        tr_used = sem("head_transposed_read")
        gate_done = sem("gate_ready")
        sm_a = sem("small_from_dve")
        sm_b = sem("small_from_act")
        gc_ready = sem("decay_sums_ready")
        gb_ready = sem("decay_rows_ready")
        d0_ready = sem("decay_differences_ready")
        dm_ready = sem("decay_exponents_ready")
        e_ready = sem("decay_from_start_ready")
        dt_ready = sem("decay_matrix_ready")
        pat_ready = sem("decay_masked")
        pds_ready = sem("decay_strict_masked")
        qd_ready = sem("decayed_queries_ready")
        eye_ready = sem("identities_ready")
        kk_ready = sem("key_products_ready")
        kq_ready = sem("query_products_ready")
        at_ready = sem("attention_ready")
        nl_ready = sem("lower_ready")
        a_ready = sem("level_a_ready")
        am_ready = sem("level_a_copied")
        b_ready = sem("level_b_ready")
        t_ready = sem("inverse_ready")
        ks_ready = sem("state_keys_ready")
        y_ready = sem("residual_values_ready")
        ty_ready = sem("solved_ready")
        vn_ready = sem("new_values_ready")
        kdm_ready = sem("decayed_keys_ready")
        od_ready = sem("outputs_ready")
        s_done = sem("state_product_ready")
        bo_ready = sem("outputs_copied")
        st_upd = sem("states_updated")
        og_ready = sem("head_normed_by_root")
        og2_ready = sem("gated_output_ready")
        w2_zero = sem("gate_weights_cleared")
        w2_loaded = sem("gate_weights_loaded")
        low_copied = sem("ranks_copied")
        low_t = sem("ranks_transposed")
        low_ready = sem("ranks_ready")
        lg_ready = sem("logits_ready")
        l1_ready = sem("log1p_ready")
        la_ready = sem("log_decay_ready")
        cum_ready = sem("cumulated_ready")
        cb_ready = sem("cumulated_copied")
        dx_ready = sem("exponents_ready")
        f_ready = sem("factors_ready")
        qf_ready = sem("factored_queries_ready")
        kf_ready = sem("factored_keys_ready")
        lv_ready = sem("level_product_ready")
        lv_used = sem("level_product_read")
        el_ready = sem("tile_decay_ready")
        x_fin = sem("x_final")
        x_out = sem("x_out_copied")
        rot_used = sem("rotated_used")
        own = {e: sem(f"{e}_step") for e in ("sp", "act", "pe", "dve", "pool")}
        gates = {e: sem(f"{e}_turn") for e in ("sp", "act", "pe", "dve", "pool")}
        q_copied = sem("projection_copied")
        rot_ready = sem("rotated_ready")
        rope_done = sem("rope_done")
        kd_ready = sem("k_ready")
        v_ready = sem("v_ready")
        score_ready = sem("scores_ready")
        nm_ready = sem("maximum_ready")
        exp_done = sem("exp_done")
        p_ready = sem("p_ready")
        pt_ready = sem("pt_ready")
        pts_ready = sem("pt_copied")
        pv_done = sem("pv_done")
        oh_ready = sem("o_hi_ready")
        o_ready = sem("o_ready")
        sink_loaded = sem("sink_loaded")
        sink_ready = sem("sink_ready")

        KIND = ["attn", "gdn", "gla", "attn"]
        last = lambda l: l == DEPTH - 1
        toks = lambda l: slice(CTX if last(l) else 0, TOK)
        seqs = lambda l: (1,) if last(l) else (0, 1)
        half = lambda s: slice(s * CTX, s * CTX + 256)
        ident = con[:, K_ID:K_ID + P]
        ones = con[:, K_ONE:K_ONE + P]
        meanw = con[:, K_MEAN:K_MEAN + P]
        column = lambda W, c: W[:, c:c + 256].rearrange("(k p) n -> p k n", p=P)
        k8 = lambda t: t.rearrange("p (k n) -> p k n", k=KT)

        block = ctx.enter_context(nc.Block())

        @block.sync
        def _(eng):
            sp = Engine(eng, own["sp"], gates["sp"])
            unit = [0]

            def load(src, ks=KT):
                s = unit[0] % 2
                if unit[0] >= 2:
                    eng.wait_ge(w_split, sp.next(w_split, 4))
                    sp.stand()
                dst = w_raw[:, s, :].rearrange("p (k n) -> p k n", k=ks)
                eng.dma_start(dst, src).then_inc(w_loaded[s], 16)
                unit[0] += 1

            def load_ada(n):
                if n >= ADA_FIRST + 2:
                    eng.wait_ge(ada_summed, sp.next(ada_summed, 2))
                eng.dma_start(k8(ada_w[:, n % 2, :]), column(a["ada_w"][0], n * 256)).then_inc(ada_loaded[n % 2], 16)

            eng.dma_start(con[:], a["consts"]).then_inc(s_con, 16)
            eng.dma_start(sink[:].rearrange("p a b -> p (a b)"),
                          a["attn_sink"].rearrange("(o s) h -> o (s h)", o=1).to_broadcast([P, 2 * A_HEADS])).then_inc(s_con, 16)
            for n, w in enumerate((a["gdn_a_log"], a["gdn_dt_bias"])):
                eng.dma_start(gdp[:, n, :], w.rearrange("o d h -> o (d h)").to_broadcast([P, 2 * B_HEADS])).then_inc(s_con, 16)
            eng.dma_start(msk_f[:].rearrange("p a b -> p (a b)"), a["masks"]).then_inc(s_con, 16)
            rowv = lambda t, pat: t.rearrange(pat, p=P)
            small = [(0, 0, rowv(a["ada_b"][0:2], "l (r p) -> (l r) p")), (1, 0, rowv(a["ada_b"][2:4], "l (r p) -> (l r) p")),
                     (2, 0, rowv(a["ln_g"], "l w (r p) -> (l w r) p")), (2, 64, rowv(a["ln_b"], "l w (r p) -> (l w r) p"))]
            cw = rowv(a["ffn_conv_w"], "l k (r p) -> (l k r) p")
            small += [(3, 0, cw[0:128]), (4, 0, cw[128:256]), (5, 0, cw[256:264]), (5, 8, rowv(a["ffn_conv_b"], "l (r p) -> (l r) p")),
                      (5, 96, rowv(a["c_ctx"], "(r p) -> r p")), (5, 104, rowv(a["c"], "b (r p) -> (b r) p")),
                      (6, 0, rowv(a["gdn_conv_w"][0], "k (r p) -> (k r) p")), (6, 72, a["gdn_norm_w"]),
                      (6, 73, rowv(a["gla_norm_w"], "a (r p) -> (a r) p"))]
            for t, r0, src in small:
                eng.dma_start(rows[r0:r0 + src.shape[0], t, :], src).then_inc(s_con, 16)
            eng.dma_start(xin[:, 0:2, :], a["ctx"][0].rearrange("(t p) d -> p t d", p=P)).then_inc(s_in, 16)
            eng.dma_start(xin[:, 2:4, :], a["x"][0].rearrange("(t p) d -> p t d", p=P)).then_inc(s_in, 16)
            for n in range(ADA_FIRST):
                if n >= ADA_SLOTS:
                    eng.wait_ge(ada_done, sp.next(ada_done))
                eng.dma_start(k8(ada_0[:, n % ADA_SLOTS, :]), column(a["ada_w"][0], n * 256)).then_inc(ada_0_loaded[n % ADA_SLOTS], 16)
            for l in range(LAYERS):
                slot = l // 3
                if l > 0:
                    sp.skip(u_ready, 2 * KT)
                if KIND[l] == "attn":
                    for n in range(6):
                        load(column(a["attn_w_qkv"][slot], n * 256))
                    wo = a["attn_w_o"][slot]
                if l == 0:
                    eng.wait_ge(ada_done, sp.next(ada_done, ADA_SLOTS))
                    load_ada(ADA_FIRST)
                    load_ada(ADA_FIRST + 1)
                    for n in range(2):
                        load(column(wo, n * 256))
                    for n in range(ADA_FIRST + 2, ADA_UNITS):
                        load_ada(n)
                if KIND[l] == "gdn":
                    w = a["gdn_w_in"][0]
                    for n in range(2):
                        load(column(w, n * 256))
                    eng.wait_ge(u_ready, sp.next(u_ready, KT))
                    sp.skip(u_ready, -KT)
                    eng.dma_start(tw[:], w[:, 4096:].rearrange("(k p) n -> p k n", p=P)).then_inc(tail_loaded, 16)
                    for n in range(2, 16):
                        load(column(w, n * 256))
                    wo = a["gdn_w_o"][slot]
                if KIND[l] == "gla":
                    w = a["gla_w_in"][0]
                    for n in range(2):
                        load(column(w, n * 256))
                    eng.wait_ge(w2_zero, sp.next(w2_zero))
                    eng.dma_start(ctw[:], w[:, 3072:].rearrange("(k p) n -> p k n", p=P)).then_inc(tail_loaded, 16)
                    for z in range(2):
                        eng.dma_start(cw2[z * C_RANK:(z + 1) * C_RANK, z * C_K:(z + 1) * C_K], a["gla_w_gate2"][0, z]).then_inc(w2_loaded, 16)
                    eng.dma_start(cw2[32:33, :], a["gla_gate_b"].rearrange("o z d -> o (z d)")).then_inc(w2_loaded, 16)
                    for n in (2, 3, 8, 9, 10, 11, 4, 5, 6, 7):
                        load(column(w, n * 256))
                    wo = a["gla_w_o"][slot]
                for n in range(2 if l == 0 else 0, 4):
                    load(column(wo, n * 256))
                up = a["ffn_w_up"][l]
                with sp.loop(FT // 2, {w_split: 8}) as i:
                    load(up[:, bass.ds(i * 256 + D_FF, 256)].rearrange("(k p) n -> p k n", p=P))
                    load(up[:, bass.ds(i * 256, 256)].rearrange("(k p) n -> p k n", p=P))
                down = a["ffn_w_down"][l]
                load(down[0:256, :].rearrange("(f p) n -> p f n", p=P), 2)
                with sp.loop(4, {w_split: 8}) as i:
                    load(down[bass.ds(i * 512 + 256, 256), :].rearrange("(f p) n -> p f n", p=P), 2)
                    load(down[bass.ds(i * 512 + 512, 256), :].rearrange("(f p) n -> p f n", p=P), 2)
                load(down[9 * 256:10 * 256, :].rearrange("(f p) n -> p f n", p=P), 2)
                load(down[10 * 256:11 * 256, :].rearrange("(f p) n -> p f n", p=P), 2)
            for t in range(2):
                eng.wait_ge(x_out, sp.next(x_out))
                eng.dma_start(out[0, t * P:(t + 1) * P, :], xout[:, t, :]).then_inc(out_stored, 16)
            eng.wait_ge(out_stored, 32)

        @block.gpsimd
        def _(eng):
            pool = Engine(eng, own["pool"], gates["pool"])
            unit = [0]

            def split(n=1):
                for _ in range(n):
                    s = unit[0] % 2
                    eng.wait_ge(w_loaded[s], pool.next(w_loaded[s], 16))
                    pool.stand()
                    for q in range(4):
                        if unit[0] > 0:
                            eng.wait_ge(w_done, pool.next(w_done))
                            pool.stand()
                        src = w_raw[:, s, q * PIECE:(q + 1) * PIECE]
                        eng.tensor_scalar(w_hi[:, q, :], src, 1.0, 0.0, ALU.mult, ALU.add).then_inc(pool.own, pool.step())
                        eng.wait_ge(pool.own, pool.count())
                        pool.stand()
                        eng.tensor_tensor(w_lo[:, q, :], src, w_hi[:, q, :].bitcast(F32), ALU.subtract).then_inc(w_split, 1)
                    unit[0] += 1

            def new_x(l, w):
                for t in range(KT):
                    eng.wait_ge(uhi_ready, pool.next(uhi_ready))
                    T = toks(l)
                    eng.tensor_scalar(x[:, t, T], x[:, t, T], vec[:, LNG(l, w, t):LNG(l, w, t) + 1],
                                      vec[:, LNB(l, w, t):LNB(l, w, t) + 1], ALU.mult, ALU.add).then_inc(x_ready, 1)

            def delta_net():
                masks = [(K_TRI, K_STR), (K_TRIB, K_STRB)]
                wide = lambda k: con[:, k:k + P].unsqueeze(1).to_broadcast([P, 4, P])
                eng.wait_ge(sm_a, pool.next(sm_a, 6))
                for s in range(TT):
                    for hg in range(2):
                        if (s, hg) != (0, 0):
                            eng.wait_ge(s_done, pool.next(s_done, 2))
                        for d in range(2):
                            Dm, NLm = bt[d][0], bt[d][3]
                            eng.wait_ge(dt_ready, pool.next(dt_ready))
                            eng.tensor_tensor(NLm[:], Dm[:], wide(masks[d][1]), ALU.mult).then_inc(pds_ready, 1)
                        for d in range(2):
                            Dm, AT = bt[d][0], bt[d][2]
                            eng.tensor_tensor(AT[:], Dm[:], wide(masks[d][0]), ALU.mult).then_inc(pat_ready, 1)
                        for d in range(2):
                            tl = s if d == 0 else s ^ 1
                            E = bt[d][1]
                            eng.wait_ge(e_ready, pool.next(e_ready))
                            eng.tensor_tensor(E[:], E[:], bq[:, hg * 4:hg * 4 + 4, tl * P:(tl + 1) * P], ALU.mult).then_inc(qd_ready, 1)
                eng.wait_ge(s_done, pool.next(s_done, 2))

            def linear_attention():
                for d in range(2):
                    for n in range(C_HEADS * (NL + 2)):
                        h, v = divmod(n, NL + 2)
                        eng.wait_ge(f_ready, pool.next(f_ready))
                        if (d, n) == (0, 0):
                            eng.memset(cqf[:], 0.0).then_inc(pool.own, pool.step())
                            eng.memset(ckf[:], 0.0).then_inc(pool.own, pool.step())
                            eng.wait_ge(pool.own, pool.count())
                        if n == 0 and d == 1:
                            eng.wait_ge(s_done, pool.next(s_done, 2 * TT))
                        if (d, n) >= (0, 2):
                            eng.wait_ge(lv_ready, pool.next(lv_ready))
                        F = cF[:, n % 2, :]
                        if v == 0:
                            ins = eng.tensor_tensor(cqe[:, h, :], cq[:, h, :], F, ALU.mult)
                        elif v == 1:
                            ins = eng.tensor_tensor(ckf[:, n % 2, :], ck[:, h, :], F, ALU.mult)
                        else:
                            b = LEVELS[NL + 1 - v]
                            part = lambda t: t.rearrange("p (n z b) -> p n z b", z=2, b=b)[:, :, 1 - d, :]
                            ins = eng.tensor_tensor(part(cqf[:, n % 2, :]), part(cq[:, h, :]), part(F), ALU.mult)
                        ins.then_inc(qf_ready, 1)
                        if v >= 2:
                            part = lambda t: t.rearrange("p (n z b) -> p n z b", z=2, b=b)[:, :, d, :]
                            eng.tensor_tensor(part(ckf[:, n % 2, :]), part(ck[:, h, :]), part(F), ALU.mult).then_inc(kf_ready, 1)
                eng.wait_ge(lv_ready, pool.next(lv_ready, 2))
                eng.wait_ge(s_done, pool.next(s_done, 2 * TT))

            split(1)
            pool.skip(uhi_ready, KT)
            for l in range(LAYERS):
                if KIND[l] == "attn":
                    split(5)
                if KIND[l] == "gdn":
                    split(15)
                    delta_net()
                if KIND[l] == "gla":
                    split(11)
                    linear_attention()
                split(5)
                new_x(l, 0)
                with pool.loop((FT + FT // 2 - 1) // 2, {w_loaded[0]: 16, w_loaded[1]: 16, w_done: 8, own["pool"]: 8}):
                    split(2)
                if l + 1 < LAYERS:
                    split(1)
                    new_x(l, 1)

        @block.scalar
        def _(eng):
            act = Engine(eng, own["act"], gates["act"])

            def make_u(l_aff, w, l):
                S = toks(l)
                for t in range(KT):
                    if first_u[0] < 2:
                        first_u[0] += 1
                    else:
                        eng.wait_ge(u_ready, act.next(u_ready))
                    eng.wait_ge(xh_ready, act.next(xh_ready))
                    for s in seqs(l):
                        eng.activation(u32[:, t % 2, half(s)], x[:, t, half(s)], ACT.Identity,
                                                bias=aff[:, l_aff, 2 * w + 1, t, s:s + 1],
                                                scale=aff[:, l_aff, 2 * w, t, s:s + 1]).then_inc(act.own, act.step())
                    eng.wait_ge(act.own, act.count())
                    eng.activation(u_hi[:, t, S], u32[:, t % 2, S], ACT.Copy).then_inc(uhi_ready, 1)

            first_u = [0]

            def attention(l):
                slot, T = l // 3, toks(l)
                qts = range(T.start // P, TT)
                for n in range(5):
                    eng.wait_ge(w_done, act.next(w_done, 4))
                    for m in range(2):
                        b = bank[(n % 2) * 2 + m]
                        dst, S = (aq[:, 2 * n + m, T], T) if n < 4 else (ak[:, m, :], slice(0, TOK))
                        eng.activation(dst, b[:, S], ACT.Copy).then_inc(q_copied, 1)
                act.skip(w_done, 4)
                eng.wait_ge(rope_done, act.next(rope_done, 10))
                for gi in range(A_KV):
                    for r in (0, 64):
                        ins = eng.activation(akd[r:r + 64, gi, :], ak[64 * (gi % 2):64 * (gi % 2) + 64, gi // 2, :], ACT.Copy)
                        if (gi, r) == (A_KV - 1, 64):
                            ins.then_inc(kd_ready, 1)
                items = [(h, qt) for t in range(KT) for h in (2 * t, 2 * t + 1) for qt in qts]
                keys = lambda qt: TT if qt >= 2 else 2
                per_pair = 2 * len(qts)

                def o_hi(t):
                    eng.wait_ge(pv_done, act.next(pv_done, per_pair))
                    eng.activation(u_hi[:, t, T], bank[4 + t % 2][:, T], ACT.Copy).then_inc(oh_ready, 1)

                for i in range(len(items) + 4):
                    if i < len(items):
                        h, qt = items[i]
                        NK = keys(qt) * P
                        eng.wait_ge(nm_ready, act.next(nm_ready))
                        eng.activation(ast[:, 2, i % 4:i % 4 + 1], sink[:, slot, h:h + 1], ACT.Exp,
                                                bias=ast[:, 1, i % 4:i % 4 + 1]).then_inc(act.own, act.step())
                        eng.activation(ap_[:, i % 4, 0:NK], bank[i % 2][:, 0:NK], ACT.Exp, scale=A_SCALE,
                                       bias=ast[:, 1, i % 4:i % 4 + 1], accum_out=ast[:, 3, i % 4:i % 4 + 1]).then_inc(exp_done, 1)
                    if 0 <= i - 2 < len(items):
                        j = i - 2
                        n = keys(items[j][1]) * P
                        if j >= 2:
                            eng.wait_ge(pv_done, act.next(pv_done))
                        eng.wait_ge(pt_ready, act.next(pt_ready))
                        eng.activation(apt[:, j % 2, 0:n], bank[2 + j % 2][:, 0:n], ACT.Copy).then_inc(pts_ready, 1)
                    if i >= 4 and (i - 3) % per_pair == 0:
                        done = (i - 3) // per_pair
                        seen_pv = max(0, min(len(items), i - 1) - 2)
                        act.skip(pv_done, -seen_pv)
                        act.skip(pv_done, (done - 1) * per_pair)
                        o_hi(done - 1)
                        act.skip(pv_done, seen_pv - done * per_pair)
                act.skip(pv_done, 2)

            def tail_hi():
                eng.wait_ge(tail_loaded, act.next(tail_loaded, 16))
                eng.activation(tw_hi[:], tw[:], ACT.Copy).then_inc(tail_h, 1)

            def delta_net():
                tail_hi()
                for n in range(13):
                    if n < 12:
                        eng.wait_ge(w_done, act.next(w_done, 4))
                        if n >= 9:
                            eng.wait_ge(hv_ready, act.next(hv_ready, 2))
                        for m in range(2):
                            j = 2 * n + m
                            eng.activation(bc[:, m, :], bank[(n % 2) * 2 + m][:], ACT.Identity,
                                           scale=vec[:, GDNCW(1) + j:GDNCW(1) + j + 1]).then_inc(conv_c, 1)
                        for m in range(2):
                            j = 2 * n + m
                            eng.wait_ge(conv_done, act.next(conv_done))
                            dst = (bq, bk, bo)[j // 8][:, j % 8, :]
                            ins = eng.activation(dst, bc[:, m, :], ACT.Silu)
                            if j < 16:
                                ins.then_inc(act.own, act.step())
                            else:
                                ins.then_inc(hv_ready, 1)
                    if 1 <= n <= 8:
                        for m in range(2):
                            eng.wait_ge(ss_ready, act.next(ss_ready))
                            eng.activation(brn[:, m, :], bank[4 + m][:], ACT.Sqrt, bias=con[:, K_COL + 1:K_COL + 2]).then_inc(rt_ready, 1)
                    if n < 8:
                        eng.wait_ge(act.own, act.count())
                        for m in range(2):
                            j = 2 * n + m
                            eng.activation(bsq[:, m, :], (bq, bk)[j // 8][:, j % 8, :], ACT.Square).then_inc(sq_h, 1)
                for n in range(4):
                    eng.wait_ge(w_done, act.next(w_done, 4))
                    for m in range(2):
                        eng.activation(bg[:, 2 * n + m, :], bank[(n % 2) * 2 + m][:], ACT.Silu).then_inc(gate_done, 1)
                eng.wait_ge(sm_a, act.next(sm_a))
                eng.activation(b_e[:], b_ax[:], ACT.Exp, scale=-1.0).then_inc(act.own, act.step())
                eng.activation(gdp[:, 0, :], gdp[:, 0, :], ACT.Exp).then_inc(act.own, act.step())
                eng.wait_ge(act.own, act.count())
                eng.activation(b_ln[:], b_e[:], ACT.Ln, bias=1.0).then_inc(act.own, act.step())
                eng.activation(b_beta[:], b_beta[:], ACT.Sigmoid).then_inc(sm_b, 1)
                eng.wait_ge(sm_a, act.next(sm_a, 2))
                eng.activation(b_negc[:], b_ngc[:], ACT.Exp, scale=-1.0).then_inc(act.own, act.step())
                eng.activation(b_kd[:], b_kd[:], ACT.Exp).then_inc(act.own, act.step())
                eng.activation(b_egl[:], bank[5][:, 64:128].rearrange("p (t h) -> p t h", t=TT), ACT.Exp).then_inc(sm_b, 1)

                def identities(d):
                    eye = ident.unsqueeze(1).to_broadcast([P, 4, P])
                    eng.activation(bt[d][4][:], eye, ACT.Copy).then_inc(act.own, act.step())
                    eng.activation(bt[d][5][:], eye, ACT.Copy).then_inc(eye_ready, 1)

                eng.wait_ge(sm_a, 6)
                for d in range(2):
                    identities(d)
                for s in range(TT):
                    for hg in range(2):
                        for d in range(2):
                            Dm, E, AT, NLm, Tm, TTm, Am = bt[d]
                            A_, B_, C_ = (bank[3 * d + k] for k in range(3))
                            if (s, hg) != (0, 0):
                                eng.wait_ge(s_done, act.next(s_done))
                            eng.wait_ge(d0_ready, act.next(d0_ready))
                            eng.activation(E[:].rearrange("p a b -> p (a b)"), A_[:], ACT.Exp).then_inc(e_ready, 1)
                            eng.wait_ge(dm_ready, act.next(dm_ready))
                            eng.activation(Dm[:], Dm[:], ACT.Exp).then_inc(dt_ready, 1)
                        for lv in range(1, NL):
                            for d in range(2):
                                eng.wait_ge(a_ready, act.next(a_ready))
                                eng.activation(bt[d][6][:].rearrange("p a b -> p (a b)"), bank[3 * d][:], ACT.Copy).then_inc(am_ready, 1)
                        for d in range(2):
                            if (s, hg) != (TT - 1, 1):
                                eng.wait_ge(ty_ready, act.next(ty_ready))
                                identities(d)
                eng.wait_ge(s_done, act.next(s_done, 2))

            def linear_attention():
                eng.wait_ge(tail_loaded, act.next(tail_loaded, 16))
                eng.activation(tw_hi[:], ctw[:], ACT.Copy).then_inc(tail_h, 1)
                for n in range(8):
                    eng.wait_ge(w_done, act.next(w_done, 4))
                    for m in range(2):
                        b = bank[(n % 2) * 2 + m]
                        if n < 2:
                            ins = eng.activation(cq[:, 2 * n + m, :], b[:], ACT.Copy, scale=C_KD ** -0.5)
                        elif n < 4:
                            ins = eng.activation(ck[:, 2 * n - 4 + m, :], b[:], ACT.Copy)
                        else:
                            ins = eng.activation(cg[:, 2 * n - 8 + m, :], b[:], ACT.Silu)
                        ins.then_inc(q_copied, 1)
                act.skip(w_done, 16)
                for i in range(8):
                    r = clg[:, i % 3, :]
                    if i >= 3:
                        eng.wait_ge(la_ready, act.next(la_ready))
                    eng.wait_ge(lg_ready, act.next(lg_ready))
                    eng.activation(r, bank[i % 4][:], ACT.Abs).then_inc(act.own, act.step())
                    eng.wait_ge(act.own, act.count())
                    eng.activation(r, r, ACT.Exp, scale=-1.0).then_inc(act.own, act.step())
                    eng.wait_ge(act.own, act.count())
                    eng.activation(r, r, ACT.Ln, bias=1.0).then_inc(l1_ready, 1)
                eng.wait_ge(la_ready, act.next(la_ready, 3))
                for d in range(2):
                    for n in range(C_HEADS * (NL + 2)):
                        h, v = divmod(n, NL + 2)
                        B, F = cb[:, h % 2, :], cF[:, n % 2, :]
                        if v == 0:
                            eng.wait_ge(cum_ready, act.next(cum_ready))
                            if (d, h) > (0, 1):
                                eng.wait_ge(act.own, act.count())
                            eng.activation(B, bank[2 + h % 2][:], ACT.Copy, scale=1.0 / C_TAU).then_inc(cb_ready, 1)
                            eng.wait_ge(cb_ready, act.next(cb_ready))
                            end = B.rearrange("p (t n) -> p t n", t=TT)[:, :, (P - 1) * (1 - d)]
                            if h == 0 and d == 1:
                                eng.wait_ge(s_done, act.next(s_done, 2 * TT))
                                eng.wait_ge(st_upd, act.next(st_upd, 2 * TT))
                            eng.activation(cel[:, h, :], end, ACT.Exp).then_inc(el_ready, 1)
                        eng.wait_ge(dx_ready, act.next(dx_ready))
                        eng.activation(F, B if v == 0 else F, ACT.Exp).then_inc(f_ready, 1)
                        if v == 0:
                            eng.wait_ge(f_ready, act.next(f_ready))
                        else:
                            act.skip(f_ready)
                eng.wait_ge(s_done, act.next(s_done, 2 * TT))
                eng.wait_ge(st_upd, act.next(st_upd, 2 * TT))

            def head_finish(o, gate, heads, dim):
                for i in range(len(heads) + 2):
                    if 0 <= i - 1 < len(heads):
                        j = i - 1
                        if j >= 2:
                            eng.wait_ge(og_ready, act.next(og_ready))
                        eng.wait_ge(ss_ready, act.next(ss_ready))
                        eng.activation(sq[:, j % 2, :], bank[4 + j % 2][:], ACT.Sqrt, bias=con[:, K_COL + 2:K_COL + 3],
                                       scale=1.0 / dim).then_inc(rt_ready, 1)
                    if i < len(heads):
                        for m, t in enumerate(heads[i]):
                            eng.activation(sq[:, 2 + m, :], o[:, t, :], ACT.Square).then_inc(sq_ready, 1)
                    if i - 2 >= 0:
                        for t in heads[i - 2]:
                            eng.wait_ge(og2_ready, act.next(og2_ready))
                            eng.activation(u_hi[:, t, :], o[:, t, :], ACT.Copy).then_inc(oh_ready, 1)
                eng.wait_ge(og_ready, act.next(og_ready, 2))

            def load_ada(l, slot, c):
                src = a["ada_w"][l][:, bass.ds(c, 256)].rearrange("(k p) n -> p k n", p=P)
                eng.dma_start(k8(ada_w[:, slot, :]), src).then_inc(ada_loaded[slot], 16)

            def norm_stats(l, w):
                S = toks(l)
                for t in range(KT):
                    eng.wait_ge(c_ready, act.next(c_ready))
                    if t >= 4:
                        eng.wait_ge(sq_used, act.next(sq_used))
                    eng.activation(sq[:, t % 4, S], x[:, t, S], ACT.Square).then_inc(sq_ready, 1)
                act.skip(sq_used, 3)
                eng.wait_ge(act.own, act.count())
                eng.activation(warm[:], con[:, K_COL:K_COL + 1], ACT.Sqrt).then_inc(act.own, act.step())
                eng.wait_ge(var_ready, act.next(var_ready))
                eng.activation(rstd[:, S], bank[STAT[w][1]][:, S], ACT.Sqrt, bias=con[:, K_COL:K_COL + 1]).then_inc(std_ready, 1)

            eng.wait_ge(vec_ready, act.next(vec_ready, ROWT))
            eng.activation(sT[:].rearrange("p k s -> p s k"), vec[:, CVEC:CVEC + 16].rearrange("p (s k) -> p s k", s=2),
                           ACT.Silu).then_inc(st_ready, 1)
            eng.wait_ge(mod_ready, act.next(mod_ready))
            make_u(0, 0, 0)
            for l in range(LAYERS):
                T = toks(l)
                if KIND[l] == "attn":
                    attention(l)
                if KIND[l] == "gdn":
                    delta_net()
                    head_finish(bo, bg, [(h,) for h in range(B_HEADS)], B_HD)
                if KIND[l] == "gla":
                    act.skip(st_upd, 16)
                    linear_attention()
                    head_finish(co, cg, [(2 * h, 2 * h + 1) for h in range(C_HEADS)], C_VD)
                act.skip(w_done, 16)
                more = l + 1 < LAYERS
                if more:
                    eng.wait_ge(ada_done, act.next(ada_done, ADA_UNITS))
                    if l == 0:
                        act.skip(ada_summed, 2 * (ADA_UNITS - ADA_FIRST))
                    load_ada(l + 1, 0, 0)
                    load_ada(l + 1, 1, 256)
                norm_stats(l, 0)
                if l == 0:
                    eng.wait_ge(mod_ready, act.next(mod_ready))
                make_u(l, 1, l)
                if more:
                    for n in range(2):
                        eng.wait_ge(ada_done, ADA_UNITS * (l + 1) + n + 1)
                        load_ada(l + 1, n, 512 + n * 256)

                def up_pair(i, load):
                    eng.wait_ge(g_done, act.next(g_done, 2))
                    act.stand()
                    eng.wait_ge(w_done, act.next(w_done, 4))
                    act.stand()
                    for m in range(2):
                        f = i * 2 + m
                        eng.activation(cv[:, m, T], bank[m][:, T], ACT.Identity,
                                       bias=vec[:, bass.ds(f + CONVB(l), 1)],
                                       scale=vec[:, bass.ds(f + CONVW(l, 1), 1)]).then_inc(conv_c, 1)
                    if load:
                        eng.wait_ge(ada_summed, act.next(ada_summed, 2))
                        act.stand()
                        load_ada(l + 1, 0, i * 512 + 1024)
                    for m in range(2):
                        eng.wait_ge(conv_done, act.next(conv_done))
                        act.stand()
                        eng.activation(cv[:, m, T], cv[:, m, T], ACT.Silu).then_inc(silu_done, 1)
                    if load:
                        eng.wait_ge(ada_summed, act.next(ada_summed, 2))
                        act.stand()
                        load_ada(l + 1, 1, i * 512 + 1280)
                    act.skip(w_done, 4)

                per = {w_done: 8, conv_done: 2, g_done: 2}
                if more:
                    per[ada_summed] = 4
                with act.loop(FT // 2 - 1, per) as i:
                    up_pair(i, more)
                up_pair(FT // 2 - 1, False)
                if more:
                    act.skip(ada_summed, 4)

                def g_hi(slot, gf, wait):
                    if wait:
                        eng.wait_ge(w_done, act.next(w_done, 2))
                        act.stand()
                    eng.activation(gs_hi[:, slot, T], gf, ACT.Copy).then_inc(gs_h, 1)

                eng.wait_ge(g_done, act.next(g_done, 2))
                act.skip(g_done, -2)
                for f in range(4):
                    g_hi(f, g[:, f, T], False)
                with act.loop(4, {w_done: 8}) as i:
                    for j in range(4):
                        g_hi(j, g[:, bass.ds(i * 4 + 4 + j, 1), T].rearrange("p a n -> p (a n)"), True)
                for f in range(20, FT):
                    g_hi(f % 4, g[:, f, T], True)
                act.skip(w_done, 8)
                norm_stats(l, 1)
                if l + 1 < LAYERS:
                    eng.wait_ge(mod_ready, act.next(mod_ready))
                    make_u(l + 1, 0, l)

        @block.tensor
        def _(eng):
            pe = Engine(eng, own["pe"], gates["pe"])
            ada_n = [0]

            def column_unit(hi, lo, banks, T, first=None):
                for q in range(4):
                    eng.wait_ge(w_split, pe.next(w_split))
                    pe.stand()
                    for k in (2 * q, 2 * q + 1):
                        if first:
                            first(k)
                        for m in range(2):
                            c = (k % 2) * 256 + m * P
                            for n, (w, v) in enumerate(((w_hi, lo), (w_lo, hi), (w_hi, hi))):
                                mm = eng.matmul(bank[banks[m]][:, T], w[:, q, c:c + P], v[:, k, T],
                                                start=(k == 0 and n == 0), stop=(k == KT - 1 and n == 2))
                    mm.then_inc(w_done, 1)

            def token_unit(banks):
                for q in range(4):
                    eng.wait_ge(w_split, pe.next(w_split))
                    for k in (2 * q, 2 * q + 1):
                        for t in range(TT):
                            c = (k % 2) * 256
                            for n, (w, v) in enumerate(((w_hi, u_lo), (w_lo, u_hi), (w_hi, u_hi))):
                                mm = eng.matmul(bank[banks[t]][:, 0:256], v[:, k, t * P:(t + 1) * P], w[:, q, c:c + 256],
                                                start=(k == 0 and n == 0), stop=(k == KT - 1 and n == 2))
                    mm.then_inc(w_done, 1)

            def attention(l):
                slot, T = l // 3, toks(l)
                qts = range(T.start // P, TT)

                def rotate(t, src):
                    if t >= 2:
                        eng.wait_ge(rot_used, pe.next(rot_used))
                    eng.matmul(bank[4 + t % 2][:, 0:SEQ], con[:, K_ROT:K_ROT + P], src, start=True, stop=True).then_inc(rot_ready, 1)

                for n in range(5):
                    column_unit(u_hi, u_lo, (0, 1) if n % 2 == 0 else (2, 3), T if n < 4 else slice(0, TOK),
                                first=u_tile if n == 0 else None)
                    for m in (2 * n - 2, 2 * n - 1):
                        if m >= 0:
                            eng.wait_ge(q_copied, pe.next(q_copied))
                            rotate(m, aq[:, m, CTX:])
                for m in (8, 9):
                    eng.wait_ge(q_copied, pe.next(q_copied))
                    rotate(m, ak[:, m - 8, CTX:])
                token_unit((0, 1, 2, 3))
                eng.wait_ge(kd_ready, pe.next(kd_ready))
                eng.wait_ge(v_ready, pe.next(v_ready, 4))
                items = [(h, qt) for t in range(KT) for h in (2 * t, 2 * t + 1) for qt in qts]
                keys = lambda qt: TT if qt >= 2 else 2
                for i in range(len(items) + 3):
                    if i < len(items):
                        h, qt = items[i]
                        b, r, t, NK = bank[i % 2], 64 * (h % 2), h // 2, keys(qt) * P
                        if i >= 2:
                            eng.wait_ge(exp_done, pe.next(exp_done))
                        mm = eng.matmul(b[:, 0:NK], aq[r:r + 64, t, qt * P:(qt + 1) * P], akd[r:r + 64, h // 4, 0:NK],
                                        start=True, stop=(qt < 2))
                        if qt >= 2:
                            c = 384 if qt == 2 else 256
                            mm = eng.matmul(b[:, c:c + P], ident, con[:, K_AM + (qt - 2) * P:K_AM + (qt - 1) * P],
                                            start=False, stop=True)
                        mm.then_inc(score_ready, 1)
                    if 0 <= i - 2 < len(items):
                        j = i - 2
                        h, qt = items[j]
                        if j >= 2:
                            eng.wait_ge(pts_ready, pe.next(pts_ready))
                            pe.skip(pts_ready, -1)
                        eng.wait_ge(p_ready, pe.next(p_ready))
                        for kt in range(keys(qt)):
                            mm = eng.transpose(bank[2 + j % 2][:, kt * P:(kt + 1) * P], ap_[:, j % 4, kt * P:(kt + 1) * P], ident)
                        mm.then_inc(pt_ready, 1)
                    if 0 <= i - 3:
                        j = i - 3
                        h, qt = items[j]
                        t, r = h // 2, 64 * (h % 2)
                        if h % 2 == 0 and qt == qts[0] and t >= 2:
                            eng.wait_ge(o_ready, pe.next(o_ready))
                        eng.wait_ge(pts_ready, pe.next(pts_ready))
                        n = keys(qt)
                        for kt in range(n):
                            mm = eng.matmul(bank[4 + t % 2][r:r + 64, qt * P:(qt + 1) * P], av[:, kt, h // 4 * 64:h // 4 * 64 + 64],
                                            apt[:, j % 2, kt * P:(kt + 1) * P], start=(kt == 0), stop=(kt == n - 1))
                        mm.then_inc(pv_done, 1)
                    if l == 0 and i % 4 == 2 and i >= 6:
                        if i == 6:
                            eng.wait_ge(mod_ready, pe.next(mod_ready))
                        ada_sum(2 * (ADA_FIRST + i // 4 - 1), (i // 4 - 1) % 2)
                if l == 0:
                    for n in range(2):
                        pe.skip(ada_loaded[n], 16 * (ADA_UNITS - ADA_FIRST) // 2)
                eng.wait_ge(o_ready, pe.next(o_ready, 2))
                pe.skip(rot_used, 2)
                pe.skip(exp_done, 2)

            def tail_unit():
                eng.wait_ge(tail_ready, pe.next(tail_ready))
                for t in range(TT):
                    for k in range(KT):
                        for n, (w, v) in enumerate(((tw_hi, u_lo), (tw_lo, u_hi), (tw_hi, u_hi))):
                            mm = eng.matmul(bank[6][:, t * 32:(t + 1) * 32], v[:, k, t * P:(t + 1) * P], w[:, k, :],
                                            start=(k == 0 and n == 0), stop=(k == KT - 1 and n == 2))
                mm.then_inc(tail_done, 1)

            def head_finish(heads):
                for i, tiles in enumerate(heads):
                    if i >= 2:
                        eng.wait_ge(rt_ready, pe.next(rt_ready))
                    for m, t in enumerate(tiles):
                        eng.wait_ge(sq_ready, pe.next(sq_ready))
                        mm = eng.matmul(bank[4 + i % 2][:], ones, sq[:, 2 + m, :], start=(m == 0), stop=(m == len(tiles) - 1))
                    mm.then_inc(ss_ready, 1)
                eng.wait_ge(rt_ready, pe.next(rt_ready, 2))

            def linear_attention():
                for n in range(8):
                    if n >= 2:
                        eng.wait_ge(q_copied, pe.next(q_copied, 2))
                    column_unit(u_hi, u_lo, (0, 1) if n % 2 == 0 else (2, 3), slice(0, TOK), first=u_tile if n == 0 else None)
                eng.wait_ge(q_copied, pe.next(q_copied, 4))
                tail_unit()
                token_unit((0, 1, 2, 3))
                eng.wait_ge(low_copied, pe.next(low_copied))
                for t in range(TT):
                    mm = eng.transpose(bank[7][0:C_TAIL, t * P:(t + 1) * P], clt[:, t * C_TAIL:(t + 1) * C_TAIL], ident)
                mm.then_inc(low_t, 1)
                eng.wait_ge(low_ready, pe.next(low_ready))
                token_unit((4, 5, 6, 7))
                eng.wait_ge(v_ready, pe.next(v_ready, 4))
                token_unit((0, 1, 2, 3))
                eng.wait_ge(v_ready, pe.next(v_ready, 4))
                token_unit((4, 5, 6, 7))
                eng.wait_ge(v_ready, pe.next(v_ready, 8))
                eng.wait_ge(w2_loaded, pe.next(w2_loaded, 48))
                for i in range(8):
                    t, z = divmod(i, 2)
                    if i >= 4:
                        eng.wait_ge(la_ready, pe.next(la_ready))
                    eng.matmul(bank[i % 4][:], clow[:, t * P:(t + 1) * P], cw2[:, z * C_K:(z + 1) * C_K],
                               start=True, stop=True).then_inc(lg_ready, 1)
                eng.wait_ge(la_ready, pe.next(la_ready, 4))

                def cumulate(d, h):
                    k = (K_TRI, K_TRIB)[d]
                    if (d, h) > (0, 1):
                        eng.wait_ge(cb_ready, pe.next(cb_ready))
                    for t in range(TT):
                        mm = eng.matmul(bank[2 + h % 2][:, t * P:(t + 1) * P], cla[:, t, d * C_K + h * C_KD:d * C_K + (h + 1) * C_KD],
                                        con[:, k:k + P], start=True, stop=True)
                    mm.then_inc(cum_ready, 1)

                cumulate(0, 0)
                for d in range(2):
                    for n in range(C_HEADS * (NL + 2)):
                        h, v = divmod(n, NL + 2)
                        if v == 0 and (d, h) != (1, C_HEADS - 1):
                            cumulate(*((d, h + 1) if h + 1 < C_HEADS else (1, 0)))
                        if (d, n) >= (0, 2):
                            eng.wait_ge(lv_used, pe.next(lv_used))
                        eng.wait_ge(qf_ready, pe.next(qf_ready))
                        if v >= 2:
                            eng.wait_ge(kf_ready, pe.next(kf_ready))
                        for t in range(TT):
                            tk = slice(t * P, (t + 1) * P)
                            dst = bank[n % 2][:, tk]
                            if v == 0:
                                mm = eng.matmul(dst, ck[:, h, tk], cq[:, h, tk], start=True, stop=True)
                            elif v == 1:
                                mm = eng.transpose(dst, ckf[:, n % 2, tk], ident)
                            else:
                                mm = eng.matmul(dst, ckf[:, n % 2, tk], cqf[:, n % 2, tk], start=True, stop=True)
                        mm.then_inc(lv_ready, 1)
                    eng.wait_ge(lv_used, pe.next(lv_used, 2))
                    pe.skip(lv_used, -2)
                    for s in range(TT):
                        tl = s if d == 0 else s ^ 1
                        tk = slice(tl * P, (tl + 1) * P)
                        for hp in range(2):
                            if (d, s) != (0, 0):
                                eng.wait_ge(st_upd, pe.next(st_upd))
                                eng.wait_ge(bo_ready, pe.next(bo_ready))
                            for j in range(4):
                                h, z = 2 * hp + j // 2, j % 2
                                o = bank[4 + hp][:, j * P:(j + 1) * P]
                                eng.matmul(o, cS[:, h, z * P:(z + 1) * P], cqe[:, h, tk], start=True, stop=False)
                                mm = eng.matmul(o, cvt[:, tl, h * C_VD + z * P:h * C_VD + (z + 1) * P], cAT[:, h, tk], start=False, stop=True)
                            mm.then_inc(od_ready, 1)
                            for j in range(2):
                                h = 2 * hp + j
                                mm = eng.matmul(bank[6 + hp][:, j * C_VD:(j + 1) * C_VD], ckl[:, h, tl, :], cvt[:, tl, h * C_VD:(h + 1) * C_VD],
                                                start=True, stop=True)
                            mm.then_inc(s_done, 1)
                eng.wait_ge(st_upd, pe.next(st_upd, 2))
                eng.wait_ge(bo_ready, pe.next(bo_ready, 2))
                eng.wait_ge(lv_used, pe.next(lv_used, 2))
                eng.wait_ge(cb_ready, pe.next(cb_ready, 2))

            def delta_net():
                for n in range(16 + 2):
                    if n < 16:
                        if 2 <= n < 14:
                            eng.wait_ge(conv_done, pe.next(conv_done, 2))
                        elif n >= 14:
                            eng.wait_ge(gate_done, pe.next(gate_done, 2))
                        column_unit(u_hi, u_lo, (0, 1) if n % 2 == 0 else (2, 3), slice(0, TOK), first=u_tile if n == 0 else None)
                    if 1 <= n <= 8:
                        for m in range(2):
                            if n >= 2:
                                eng.wait_ge(rt_ready, pe.next(rt_ready))
                            eng.wait_ge(sq_h, pe.next(sq_h))
                            eng.matmul(bank[4 + m][:], ones, bsq[:, m, :], start=True, stop=True).then_inc(ss_ready, 1)
                    if 10 <= n < 14:
                        for m in range(2):
                            j = 2 * (n - 2) + m - 16
                            eng.wait_ge(hv_ready, pe.next(hv_ready))
                            if n >= 11:
                                eng.wait_ge(tr_used, pe.next(tr_used))
                            for t in range(TT):
                                mm = eng.transpose(bank[6 + m][:, t * P:(t + 1) * P], bo[:, j, t * P:(t + 1) * P], ident)
                            mm.then_inc(tr_ready, 1)
                eng.wait_ge(rt_ready, pe.next(rt_ready, 2))
                eng.wait_ge(hn_ready, pe.next(hn_ready, 16))
                eng.wait_ge(tr_used, pe.next(tr_used, 2))
                eng.wait_ge(gate_done, pe.next(gate_done, 4))
                tail_unit()
                eng.wait_ge(sm_a, pe.next(sm_a, 2))
                for t in range(TT):
                    for d in range(2):
                        c = t * H2 + d * B_HEADS
                        eng.matmul(bank[5][:, c:c + B_HEADS], con[:, (K_TRI, K_TRIB)[d]:(K_TRI, K_TRIB)[d] + P],
                                   b_g[:, t, d * B_HEADS:(d + 1) * B_HEADS], start=True, stop=True)
                eng.matmul(bank[5][:, 64:128], ones, b_g[:].rearrange("p t h -> p (t h)"), start=True, stop=True).then_inc(gc_ready, 1)
                eng.wait_ge(sm_b, pe.next(sm_b, 2))
                mask_tri = (K_TRI, K_TRIB)
                for s in range(TT):
                    for hg in range(2):
                        for d in range(2):
                            tl = s if d == 0 else s ^ 1
                            tk = slice(tl * P, (tl + 1) * P)
                            if (s, hg) != (0, 0):
                                eng.wait_ge(st_upd, pe.next(st_upd))
                            for b in range(4):
                                h = hg * 4 + b
                                c = d * B_HEADS + h
                                mm = eng.matmul(bank[3 * d][:, b * P:(b + 1) * P], b_g[:, tl, c:c + 1].to_broadcast([P, P]),
                                                con[:, mask_tri[d]:mask_tri[d] + P], start=True, stop=True)
                            mm.then_inc(gb_ready, 1)
                            for b in range(4):
                                h = hg * 4 + b
                                mm = eng.matmul(bank[3 * d + 2][:, b * P:(b + 1) * P], bk[:, h, tk], bq[:, h, tk], start=True, stop=True)
                            mm.then_inc(kq_ready, 1)
                            for b in range(4):
                                h = hg * 4 + b
                                mm = eng.matmul(bank[3 * d + 1][:, b * P:(b + 1) * P], bk[:, h, tk], bk[:, h, tk], start=True, stop=True)
                            mm.then_inc(kk_ready, 1)
                        for d in range(2):
                            eng.wait_ge(nl_ready, pe.next(nl_ready))
                            eng.wait_ge(e_ready, pe.next(e_ready))
                            for b in range(4):
                                mm = eng.transpose(bank[3 * d][:, b * P:(b + 1) * P], bt[d][3][:, b, :], ident)
                            mm.then_inc(tr_ready, 1)
                        for lv in range(1, NL):
                            for d in range(2):
                                eng.wait_ge(t_ready, pe.next(t_ready))
                                for b in range(4):
                                    mm = eng.matmul(bank[3 * d][:, b * P:(b + 1) * P], bt[d][3][:, b, :], bt[d][4][:, b, :], start=True, stop=True)
                                mm.then_inc(a_ready, 1)
                            for d in range(2):
                                if lv == 1:
                                    eng.wait_ge(at_ready, pe.next(at_ready))
                                eng.wait_ge(am_ready, pe.next(am_ready))
                                Am, Tm, TTm = bt[d][6], bt[d][4], bt[d][5]
                                for b in range(4):
                                    mm = eng.matmul(bank[3 * d + 2][:, b * P:(b + 1) * P], Am[:, b, :], TTm[:, b, :], start=True, stop=True)
                                if lv < NL - 1:
                                    for b in range(4):
                                        mm = eng.matmul(bank[3 * d + 1][:, b * P:(b + 1) * P], TTm[:, b, :], Am[:, b, :], start=True, stop=True)
                                mm.then_inc(b_ready, 1)
                        for d in range(2):
                            tl = s if d == 0 else s ^ 1
                            tk = slice(tl * P, (tl + 1) * P)
                            for b in range(4):
                                h = hg * 4 + b
                                mm = eng.matmul(bank[3 * d][:, b * P:(b + 1) * P], bk[:, h, tk], bS[:, d, h, :], start=True, stop=True)
                            mm.then_inc(ks_ready, 1)
                        for d in range(2):
                            tl = s if d == 0 else s ^ 1
                            eng.wait_ge(t_ready, pe.next(t_ready))
                            for b in range(4):
                                mm = eng.transpose(bank[3 * d + 2][:, b * P:(b + 1) * P], bk[:, hg * 4 + b, tl * P:(tl + 1) * P], ident)
                            mm.then_inc(tr_ready, 1)
                        for d in range(2):
                            eng.wait_ge(y_ready, pe.next(y_ready))
                            for b in range(4):
                                mm = eng.matmul(bank[3 * d + 1][:, b * P:(b + 1) * P], bt[d][5][:, b, :], bt[d][6][:, b, :], start=True, stop=True)
                            mm.then_inc(ty_ready, 1)
                        for d in range(2):
                            Dm, E, AT, NLm, Tm, TTm, Am = bt[d]
                            if (s, hg) != (0, 0):
                                eng.wait_ge(bo_ready, pe.next(bo_ready))
                            eng.wait_ge(qd_ready, pe.next(qd_ready))
                            eng.wait_ge(vn_ready, pe.next(vn_ready))
                            for b in range(4):
                                o = bank[6 + d][:, b * P:(b + 1) * P]
                                eng.matmul(o, bS[:, d, hg * 4 + b, :], E[:, b, :], start=True, stop=False)
                                mm = eng.matmul(o, Dm[:, b, :], AT[:, b, :], start=False, stop=True)
                            mm.then_inc(od_ready, 1)
                            eng.wait_ge(kdm_ready, pe.next(kdm_ready))
                            for b in range(4):
                                mm = eng.matmul(bank[3 * d + 2][:, b * P:(b + 1) * P], NLm[:, b, :], Dm[:, b, :], start=True, stop=True)
                            mm.then_inc(s_done, 1)
                eng.wait_ge(bo_ready, pe.next(bo_ready, 2))
                eng.wait_ge(st_upd, pe.next(st_upd, 2))

            def ada_unit(j0, ring=ada_w):
                s = ada_n[0] % (2 if ring is ada_w else ADA_SLOTS)
                loaded = (ada_loaded if ring is ada_w else ada_0_loaded)[s]
                eng.wait_ge(loaded, pe.next(loaded, 16))
                pe.stand()
                for m in range(2):
                    dst = bank[6][:, bass.ds((j0 + m) * 2, 2)] if not isinstance(j0, int) else bank[6][:, (j0 + m) * 2:(j0 + m) * 2 + 2]
                    for k in range(KT):
                        mm = eng.matmul(dst, ring[:, s, k * 256 + m * P:k * 256 + (m + 1) * P], sT[:, k, :],
                                        start=(k == 0), stop=(k == KT - 1))
                mm.then_inc(ada_done, 1)
                ada_n[0] += 1

            def ada_sum(j0, slot):
                eng.wait_ge(ada_summed, pe.next(ada_summed, 2))
                pe.stand()
                for m in range(2):
                    for q in range(2):
                        mm = eng.matmul(bank[6][:, bass.ds((j0 + m) * 2 + q, 1)], acc[:, slot, q, m * P:(m + 1) * P],
                                        ones[:, 0:1], start=True, stop=True)
                mm.then_inc(ada_done, 1)

            def mean_sum(l, w, t):
                eng.wait_ge(r_ready, pe.next(r_ready))
                S = toks(l)
                mm = eng.matmul(bank[STAT[w][0]][:, S], meanw, x[:, t, S], start=(t == 0), stop=(t == KT - 1))
                if t == KT - 1:
                    mm.then_inc(mean_ready, 1)

            def variance_sums(l, w):
                S = toks(l)
                var = bank[STAT[w][1]][:, S]
                for t in range(KT):
                    eng.wait_ge(sq_ready, pe.next(sq_ready))
                    mm = eng.matmul(var, meanw, sq[:, t % 4, S], start=(t == 0), stop=(t == KT - 1))
                    mm.then_inc(var_ready if t == KT - 1 else sq_used, 1)

            def u_tile(k):
                if k not in seen:
                    seen.add(k)
                    eng.wait_ge(u_ready, pe.next(u_ready))
            seen = set()

            eng.wait_ge(s_con, pe.next(s_con, 16 * 18))
            for t in range(ROWT):
                R = ROWS[t]
                eng.transpose(bank[t][:, 0:R], rows[0:R, t, :], ident[0:R, 0:R]).then_inc(rows_t, 1)
            eng.wait_ge(s_in, pe.next(s_in, 32))
            for t in range(KT):
                if t < ROWT:
                    eng.wait_ge(vec_ready, pe.next(vec_ready))
                for j in range(TT):
                    mm = eng.transpose(bank[t][:, j * P:(j + 1) * P], xin[:, j, t * P:(t + 1) * P], ident)
                mm.then_inc(xt_done, 1)
            eng.wait_ge(xt_copied, pe.next(xt_copied, KT))
            eng.wait_ge(st_ready, pe.next(st_ready))
            for n in range(ADA_FIRST):
                ada_unit(2 * n, ada_0)
            for l in range(LAYERS):
                T = toks(l)
                seen.clear()
                if KIND[l] == "attn":
                    attention(l)
                if KIND[l] == "gdn":
                    delta_net()
                    head_finish([(h,) for h in range(B_HEADS)])
                    eng.wait_ge(o_ready, pe.next(o_ready, B_HEADS))
                if KIND[l] == "gla":
                    linear_attention()
                    head_finish([(2 * h, 2 * h + 1) for h in range(C_HEADS)])
                    eng.wait_ge(o_ready, pe.next(o_ready, KT))
                for n in range(4):
                    if n >= 2:
                        mean_sum(l, 0, 2 * n - 4)
                        mean_sum(l, 0, 2 * n - 3)
                    column_unit(u_hi, u_lo, (0, 1) if n % 2 == 0 else (2, 3), T)
                for t in range(4, KT):
                    mean_sum(l, 0, t)
                variance_sums(l, 0)
                seen.clear()
                more = l + 1 < LAYERS
                if l == 0:
                    eng.wait_ge(mod_ready, pe.next(mod_ready))
                if more:
                    for n in range(2):
                        ada_unit(2 * n)

                def up_pair(i, first=None):
                    column_unit(u_hi, u_lo, (0, 1), T, first=first)
                    if more and first is None:
                        ada_sum(i * 4 + 2, 1)
                    eng.wait_ge(g_done, pe.next(g_done, 2))
                    pe.stand()
                    column_unit(u_hi, u_lo, (2, 3), T)
                    if more:
                        ada_sum(i * 4 + 4, 0)
                    eng.wait_ge(conv_done, pe.next(conv_done, 2))
                    pe.stand()

                up_pair(0, u_tile)
                per = {w_split: 8, conv_done: 2, g_done: 2}
                if more:
                    per[ada_summed] = 4
                with pe.loop(FT // 2 - 1, per) as i:
                    up_pair(i + 1)
                if more:
                    ada_sum(2 * ADA_UNITS - 2, 1)
                    for n in range(2):
                        pe.skip(ada_loaded[n], 16 * (FT // 2))
                    eng.wait_ge(mod_ready, pe.next(mod_ready))
                eng.wait_ge(g_done, pe.next(g_done, 2))
                pe.skip(g_done, -2)

                def down_unit(slots, start, stop):
                    for q in range(4):
                        eng.wait_ge(w_split, pe.next(w_split))
                        pe.stand()
                        if q % 2 == 0:
                            eng.wait_ge(gs_ready, pe.next(gs_ready))
                            pe.stand()
                        s = slots[q // 2]
                        for j in range(4):
                            b = (q % 2) * 4 + j
                            for n, (w, v) in enumerate(((w_hi, gs_lo), (w_lo, gs_hi), (w_hi, gs_hi))):
                                mm = eng.matmul(bank[b][:, T], w[:, q, j * P:(j + 1) * P], v[:, s, T],
                                                start=(start and q < 2 and n == 0), stop=(stop and q >= 2 and n == 2))
                        mm.then_inc(w_done, 1)

                down_unit((0, 1), True, False)
                with pe.loop(4, {w_split: 8, gs_ready: 4}):
                    down_unit((2, 3), False, False)
                    down_unit((0, 1), False, False)
                down_unit((2, 3), False, False)
                down_unit((0, 1), False, True)
                for t in range(KT):
                    mean_sum(l, 1, t)
                variance_sums(l, 1)
            for t in range(KT):
                eng.wait_ge(x_fin, pe.next(x_fin))
                for j in range(2):
                    mm = eng.transpose(bank[j * 2 + t // 4][:, (t % 4) * P:(t % 4 + 1) * P], x[:, t, CTX + j * P:CTX + (j + 1) * P], ident)
            mm.then_inc(xt_done, 1)

        @block.vector
        def _(eng):
            dve = Engine(eng, own["dve"], gates["dve"])

            def modulation(l, parts=range(6)):
                J = slice(parts[0] * KT, (parts[-1] + 1) * KT)
                b = vec[:, ADAB(l, J.start):ADAB(l, J.stop)].unsqueeze(2).to_broadcast([P, J.stop - J.start, 2])
                src = bank[6][:, 2 * J.start:2 * J.stop].rearrange("p (j s) -> p j s", s=2)
                eng.tensor_tensor(mod[:, l, J], src, b, ALU.add).then_inc(dve.own, dve.step())
                eng.wait_ge(dve.own, dve.count())
                part = lambda n: mod[:, l, n * KT:(n + 1) * KT, :]
                for w in range(2):
                    scale, shift = (aff[:, l, 2 * w + k] for k in (0, 1))
                    if 3 * w + 2 in parts:
                        eng.tensor_scalar(gat[:, l, w], part(3 * w + 2), 1.0 / ALPHA, None, ALU.mult).then_inc(dve.own, dve.step())
                    if 3 * w + 1 not in parts:
                        continue
                    eng.tensor_scalar(scale, part(3 * w + 1), 1.0, None, ALU.add).then_inc(dve.own, dve.step())
                    pl, pw = (l - 1, 1) if w == 0 else (l, 0)
                    if pl < 0:
                        eng.tensor_copy(shift, part(0)).then_inc(dve.own, dve.step())
                        continue
                    gain = vec[:, LNG(pl, pw, 0):LNG(pl, pw, 0) + KT].unsqueeze(2).to_broadcast([P, KT, 2])
                    bias = vec[:, LNB(pl, pw, 0):LNB(pl, pw, 0) + KT].unsqueeze(2).to_broadcast([P, KT, 2])
                    eng.wait_ge(dve.own, dve.count())
                    eng.tensor_tensor(shift, scale, bias, ALU.mult).then_inc(dve.own, dve.step())
                    eng.wait_ge(dve.own, dve.count())
                    eng.tensor_tensor(shift, shift, part(3 * w), ALU.add).then_inc(dve.own, dve.step())
                    eng.tensor_tensor(scale, scale, gain, ALU.mult).then_inc(dve.own, dve.step())
                eng.wait_ge(dve.own, dve.count())
                eng.sem_inc(mod_ready, 1)

            def u_low(l, t):
                S = toks(l)
                eng.wait_ge(uhi_ready, dve.next(uhi_ready))
                eng.tensor_tensor(u_lo[:, t, S], u32[:, t % 2, S], u_hi[:, t, S].bitcast(F32), ALU.subtract).then_inc(u_ready, 1)

            def residual(l, w, t, b):
                for s in seqs(l):
                    ins = eng.scalar_tensor_tensor(x[:, t, half(s)], bank[b][:, half(s)], gat[:, l, w, t, s:s + 1],
                                                   x[:, t, half(s)], ALU.mult, ALU.add)
                    if s == 1:
                        ins.then_inc(r_ready, 1)

            def ada_products(s, ks=range(KT), free=True):
                if ks[0] == 0:
                    eng.wait_ge(ada_loaded[s], dve.next(ada_loaded[s], 16))
                    dve.stand()
                    if free:
                        eng.wait_ge(ada_done, dve.next(ada_done))
                        dve.stand()
                for k in ks:
                    if k > 0:
                        eng.wait_ge(dve.own, dve.count())
                        dve.stand()
                    for q in range(2):
                        wk, c = ada_w[:, s, k * 256:(k + 1) * 256], sT[:, k, q:q + 1]
                        if k == 0:
                            eng.tensor_scalar(acc[:, s, q, :], wk, c, None, ALU.mult).then_inc(dve.own, dve.step())
                        elif k < KT - 1:
                            eng.scalar_tensor_tensor(acc[:, s, q, :], wk, c, acc[:, s, q, :],
                                                     ALU.mult, ALU.add).then_inc(dve.own, dve.step())
                        else:
                            eng.scalar_tensor_tensor(acc[:, s, q, :], wk, c, acc[:, s, q, :],
                                                     ALU.mult, ALU.add).then_inc(ada_summed, 1)

            def attention(l):
                slot, T = l // 3, toks(l)
                qts = range(T.start // P, TT)
                cos, sin = con[:, K_COS:K_COS + SEQ], con[:, K_SIN:K_SIN + SEQ]
                for t in range(10):
                    v = aq[:, t, CTX:] if t < 8 else ak[:, t - 8, CTX:]
                    eng.wait_ge(rot_ready, dve.next(rot_ready))
                    eng.tensor_tensor(art[:, t % 2, :], bank[4 + t % 2][:, 0:SEQ], sin, ALU.mult).then_inc(rot_used, 1)
                    eng.tensor_tensor(v, v, cos, ALU.mult).then_inc(dve.own, dve.step())
                    eng.wait_ge(dve.own, dve.count())
                    eng.wait_ge(rot_used, dve.next(rot_used))
                    eng.tensor_tensor(v, v, art[:, t % 2, :], ALU.add).then_inc(rope_done, 1)
                eng.wait_ge(w_done, dve.next(w_done, 24))
                for t in range(TT):
                    eng.tensor_copy(av[:, t, :], bank[t][:, 0:256]).then_inc(v_ready, 1)
                items = [(h, qt) for t in range(KT) for h in (2 * t, 2 * t + 1) for qt in qts]
                keys = lambda qt: TT if qt >= 2 else 2
                per_pair = 2 * len(qts)
                for i in range(len(items) + 4):
                    if i < len(items):
                        h, qt = items[i]
                        mx, nm = (ast[:, k, i % 4:i % 4 + 1] for k in (0, 1))
                        eng.wait_ge(score_ready, dve.next(score_ready))
                        eng.tensor_reduce(mx, bank[i % 2][:, 0:keys(qt) * P], AX.X, ALU.max).then_inc(dve.own, dve.step())
                        eng.wait_ge(dve.own, dve.count())
                        eng.tensor_scalar(nm, mx, -A_SCALE, nsink[:, slot, h:h + 1], ALU.mult, ALU.min).then_inc(nm_ready, 1)
                    if 0 <= i - 1 < len(items):
                        j = i - 1
                        es, total, rec = (ast[:, k, j % 4:j % 4 + 1] for k in (2, 3, 4))
                        pj = ap_[:, j % 4, 0:keys(items[j][1]) * P]
                        eng.wait_ge(exp_done, dve.next(exp_done))
                        eng.tensor_tensor(rec, es, total, ALU.add).then_inc(dve.own, dve.step())
                        eng.wait_ge(dve.own, dve.count())
                        eng.reciprocal(rec, rec).then_inc(dve.own, dve.step())
                        eng.wait_ge(dve.own, dve.count())
                        eng.tensor_scalar(pj, pj, rec, None, ALU.mult).then_inc(p_ready, 1)
                    if i >= 4 and (i - 3) % per_pair == 0:
                        t = (i - 3) // per_pair - 1
                        eng.wait_ge(oh_ready, dve.next(oh_ready))
                        eng.tensor_tensor(u_lo[:, t, T], bank[4 + t % 2][:, T], u_hi[:, t, T].bitcast(F32),
                                          ALU.subtract).then_inc(o_ready, 1)
                    if l == 0 and i < 4 * (ADA_UNITS - ADA_FIRST):
                        if i == 0:
                            eng.wait_ge(u_ready, KT)
                            eng.sem_inc(gates["dve"], 1)
                        n, k = divmod(i, 4)
                        ada_products(n % 2, range(2 * k, 2 * k + 2), n >= 2)
                eng.wait_ge(rope_done, dve.next(rope_done, 10))

            def tail_low():
                eng.wait_ge(tail_h, dve.next(tail_h))
                eng.tensor_tensor(tw_lo[:], tw[:], tw_hi[:].bitcast(F32), ALU.subtract).then_inc(tail_ready, 1)

            def conv(cb, b, w0, w2, S):
                v3 = lambda t, lo, hi: t.rearrange("p (s n) -> p s n", s=2)[:, S[0]:S[-1] + 1, lo:hi]
                eng.scalar_tensor_tensor(v3(cb, 1, 256), v3(b, 0, 255), w0, v3(cb, 1, 256), ALU.mult, ALU.add).then_inc(dve.own, dve.step())
                eng.wait_ge(dve.own, dve.count())
                eng.scalar_tensor_tensor(v3(cb, 0, 255), v3(b, 1, 256), w2, v3(cb, 0, 255), ALU.mult, ALU.add).then_inc(conv_done, 1)

            def delta_net():
                tail_low()
                for n in range(14):
                    if n < 12:
                        for m in range(2):
                            j = 2 * n + m
                            eng.wait_ge(conv_c, dve.next(conv_c))
                            conv(bc[:, m, :], bank[(n % 2) * 2 + m][:], vec[:, GDNCW(0) + j:GDNCW(0) + j + 1],
                                 vec[:, GDNCW(2) + j:GDNCW(2) + j + 1], (0, 1))
                    if 1 <= n <= 8:
                        for m in range(2):
                            j = 2 * (n - 1) + m
                            eng.wait_ge(rt_ready, dve.next(rt_ready))
                            eng.reciprocal(brn[:, m, :], brn[:, m, :]).then_inc(dve.own, dve.step())
                            eng.wait_ge(dve.own, dve.count())
                            h = (bq, bk)[j // 8][:, j % 8, :]
                            eng.scalar_tensor_tensor(h, h, B_HD ** -0.5 if j < 8 else 1.0, brn[:, m, :],
                                                     ALU.mult, ALU.mult).then_inc(hn_ready, 1)
                    if n >= 10:
                        for m in range(2):
                            dst = bv[:, :, 2 * (n - 2) + m - 16, :]
                            eng.wait_ge(tr_ready, dve.next(tr_ready))
                            eng.tensor_copy(dst, bank[6 + m][:].rearrange("p (t n) -> p t n", t=TT)).then_inc(tr_used, 1)
                dve.skip(w_done, 64)
                eng.wait_ge(tail_done, dve.next(tail_done))
                raw = bank[6][:, 0:128].rearrange("p (t n) -> p t n", t=TT)
                dt = gdp[:, 1, :].unsqueeze(1).to_broadcast([P, TT, H2])
                eng.tensor_tensor(b_x[:], raw[:, :, H2:], dt, ALU.add).then_inc(dve.own, dve.step())
                eng.tensor_copy(b_beta[:], raw[:, :, 0:H2]).then_inc(dve.own, dve.step())
                eng.memset(bS[:], 0.0).then_inc(dve.own, dve.step())
                eng.wait_ge(dve.own, dve.count())
                eng.scalar_tensor_tensor(b_ax[:], b_x[:], -1.0, b_x[:], ALU.mult, ALU.max).then_inc(sm_a, 1)
                eng.wait_ge(sm_b, dve.next(sm_b))
                eng.scalar_tensor_tensor(b_g[:], b_x[:], 0.0, b_ln[:], ALU.max, ALU.add).then_inc(dve.own, dve.step())
                eng.wait_ge(dve.own, dve.count())
                ea = gdp[:, 0, :].unsqueeze(1).to_broadcast([P, TT, H2])
                eng.tensor_tensor(b_g[:], b_g[:], ea, ALU.mult).then_inc(dve.own, dve.step())
                eng.wait_ge(dve.own, dve.count())
                eng.tensor_scalar(b_g[:], b_g[:], -1.0, None, ALU.mult).then_inc(sm_a, 1)
                eng.tensor_scalar(b_nbeta[:], b_beta[:], -1.0, None, ALU.mult).then_inc(dve.own, dve.step())
                eng.wait_ge(gc_ready, dve.next(gc_ready))
                v4 = lambda t: t.rearrange("p (t h) -> p t h", t=TT)
                eng.tensor_scalar(b_ngc[:], v4(bank[5][:, 0:64]), -1.0, None, ALU.mult).then_inc(dve.own, dve.step())
                eng.wait_ge(dve.own, dve.count())
                eng.tensor_tensor(b_kd[:], v4(bank[5][:, 64:128]), b_ngc[:], ALU.add).then_inc(sm_a, 1)
                eng.wait_ge(sm_b, dve.next(sm_b))
                eng.tensor_scalar(b_negc[:], b_negc[:], -1.0, None, ALU.mult).then_inc(sm_a, 3)
                dve.skip(sm_a, 6)
                for s in range(TT):
                    for hg in range(2):
                        hs = slice(hg * 4, hg * 4 + 4)
                        flat = lambda t: t.rearrange("p a b -> p (a b)")
                        quad = lambda t: t.rearrange("p (a b) -> p a b", a=4)
                        for d in range(2):
                            tl = s if d == 0 else s ^ 1
                            Dm = bt[d][0]
                            c0 = d * B_HEADS + hg * 4
                            eng.wait_ge(gb_ready, dve.next(gb_ready))
                            eng.tensor_tensor(Dm[:], quad(bank[3 * d][:]), b_ngc[:, tl, c0:c0 + 4].unsqueeze(2).to_broadcast([P, 4, P]),
                                              ALU.add).then_inc(d0_ready, 1)
                            eng.wait_ge(d0_ready, dve.next(d0_ready))
                            eng.tensor_scalar(Dm[:], Dm[:], 0.0, None, ALU.min).then_inc(dm_ready, 1)
                        for d in range(2):
                            tl = s if d == 0 else s ^ 1
                            NLm = bt[d][3]
                            eng.wait_ge(pds_ready, dve.next(pds_ready))
                            eng.wait_ge(kk_ready, dve.next(kk_ready))
                            for b in range(4):
                                c = d * B_HEADS + hg * 4 + b
                                ins = eng.scalar_tensor_tensor(NLm[:, b, :], NLm[:, b, :], b_nbeta[:, tl, c:c + 1],
                                                               bank[3 * d + 1][:, b * P:(b + 1) * P], ALU.mult, ALU.mult)
                            ins.then_inc(nl_ready, 1)
                        for d in range(2):
                            Dm, E, AT, NLm, Tm, TTm, Am = bt[d]
                            mt = [msk[:, n0 * NL, :].unsqueeze(1).to_broadcast([P, 4, P]) for n0 in ((0, 1) if d == 0 else (1, 0))]
                            eng.wait_ge(nl_ready, dve.next(nl_ready))
                            eng.wait_ge(eye_ready, dve.next(eye_ready))
                            eng.copy_predicated(TTm[:], mt[0], NLm[:]).then_inc(dve.own, dve.step())
                            eng.wait_ge(tr_ready, dve.next(tr_ready))
                            eng.copy_predicated(Tm[:], mt[1], quad(bank[3 * d][:])).then_inc(t_ready, 1)
                        for d in range(2):
                            AT = bt[d][2]
                            eng.wait_ge(pat_ready, dve.next(pat_ready))
                            eng.wait_ge(kq_ready, dve.next(kq_ready))
                            eng.tensor_tensor(AT[:], AT[:], quad(bank[3 * d + 2][:]), ALU.mult).then_inc(at_ready, 1)
                        for lv in range(1, NL):
                            for d in range(2):
                                Tm, TTm = bt[d][4], bt[d][5]
                                mt = [msk[:, n0 * NL + lv, :].unsqueeze(1).to_broadcast([P, 4, P]) for n0 in ((0, 1) if d == 0 else (1, 0))]
                                eng.wait_ge(b_ready, dve.next(b_ready))
                                if lv < NL - 1:
                                    eng.copy_predicated(Tm[:], mt[1], quad(bank[3 * d + 1][:])).then_inc(dve.own, dve.step())
                                eng.copy_predicated(TTm[:], mt[0], quad(bank[3 * d + 2][:])).then_inc(t_ready, 1)
                        for d in range(2):
                            tl = s if d == 0 else s ^ 1
                            Am = bt[d][6]
                            eng.wait_ge(ks_ready, dve.next(ks_ready))
                            for b in range(4):
                                h = hg * 4 + b
                                c = d * B_HEADS + h
                                ins = eng.scalar_tensor_tensor(Am[:, b, :], bank[3 * d][:, b * P:(b + 1) * P], b_negc[:, tl, c:c + 1],
                                                               bv[:, tl, h, :], ALU.mult, ALU.add)
                            ins.then_inc(y_ready, 1)
                        for d in range(2):
                            tl = s if d == 0 else s ^ 1
                            c0 = d * B_HEADS + hg * 4
                            eng.wait_ge(tr_ready, dve.next(tr_ready))
                            eng.tensor_tensor(bt[d][3][:], quad(bank[3 * d + 2][:]), b_kd[:, tl, c0:c0 + 4].unsqueeze(2).to_broadcast([P, 4, P]),
                                              ALU.mult).then_inc(kdm_ready, 1)
                        for d in range(2):
                            tl = s if d == 0 else s ^ 1
                            Dm = bt[d][0]
                            c0 = d * B_HEADS + hg * 4
                            eng.wait_ge(ty_ready, dve.next(ty_ready))
                            eng.tensor_tensor(Dm[:], quad(bank[3 * d + 1][:]), b_beta[:, tl, c0:c0 + 4].unsqueeze(2).to_broadcast([P, 4, P]),
                                              ALU.mult).then_inc(vn_ready, 1)
                        for d in range(2):
                            tl = s if d == 0 else s ^ 1
                            dst = bo[:, hs, tl * P:(tl + 1) * P]
                            eng.wait_ge(od_ready, dve.next(od_ready))
                            if s % 2 == 0:
                                eng.tensor_copy(dst, quad(bank[6 + d][:])).then_inc(bo_ready, 1)
                            else:
                                eng.tensor_tensor(dst, dst, quad(bank[6 + d][:]), ALU.add).then_inc(bo_ready, 1)
                            eng.wait_ge(s_done, dve.next(s_done))
                            for b in range(4):
                                h = hg * 4 + b
                                c = d * B_HEADS + h
                                ins = eng.scalar_tensor_tensor(bS[:, d, h, :], bS[:, d, h, :], b_egl[:, tl, c:c + 1],
                                                               bank[3 * d + 2][:, b * P:(b + 1) * P], ALU.mult, ALU.add)
                            ins.then_inc(st_upd, 1)
                        dve.skip(t_ready, 2 * NL)
                eng.wait_ge(bo_ready, dve.next(bo_ready, 16))
                dve.skip(st_upd, 16)

            def linear_attention():
                eng.memset(cw2[:], 0.0).then_inc(dve.own, dve.step())
                eng.memset(clow[32:33, :], 1.0).then_inc(w2_zero, 1)
                eng.wait_ge(tail_h, dve.next(tail_h))
                eng.tensor_tensor(tw_lo[:], ctw[:], tw_hi[:].bitcast(F32), ALU.subtract).then_inc(tail_ready, 1)
                eng.wait_ge(tail_done, dve.next(tail_done))
                eng.tensor_copy(clt[:], bank[6][:, 0:TT * C_TAIL]).then_inc(low_copied, 1)
                dve.skip(w_done, 32)
                for n in range(4):
                    eng.wait_ge(w_done, dve.next(w_done, 4))
                    for t in range(TT):
                        eng.tensor_copy(cvt[:, t, n * 256:(n + 1) * 256], bank[(n % 2) * 4 + t][:, 0:256]).then_inc(v_ready, 1)
                    if n == 0:
                        eng.wait_ge(low_t, dve.next(low_t))
                        eng.tensor_copy(clow[0:C_TAIL, :], bank[7][0:C_TAIL, :]).then_inc(low_ready, 1)
                for i in range(8):
                    t, z = divmod(i, 2)
                    eng.wait_ge(l1_ready, dve.next(l1_ready))
                    eng.scalar_tensor_tensor(cla[:, t, z * C_K:(z + 1) * C_K], bank[i % 4][:], 0.0, clg[:, i % 3, :],
                                             ALU.min, ALU.subtract).then_inc(la_ready, 1)
                stages = C_HEADS * (NL + 2)
                for d in range(2):
                    eng.memset(cS[:], 0.0).then_inc(dve.own, dve.step())
                    for n in range(stages + 2):
                        if n < stages:
                            h, v = divmod(n, NL + 2)
                            B, F = cb[:, h % 2, :], cF[:, n % 2, :]
                            if (d, n) >= (0, 2):
                                eng.wait_ge(qf_ready, dve.next(qf_ready))
                                if (n - 2) % (NL + 2) >= 2:
                                    eng.wait_ge(kf_ready, dve.next(kf_ready))
                            if v == 0:
                                eng.wait_ge(cb_ready, dve.next(cb_ready))
                                eng.sem_inc(dx_ready, 1)
                            elif v == 1:
                                q = lambda t: t.rearrange("p (t n) -> p t n", t=TT)
                                c = (P - 1) * (1 - d)
                                eng.tensor_tensor(q(F), q(B)[:, :, c:c + 1].to_broadcast([P, TT, P]), q(B), ALU.subtract).then_inc(dx_ready, 1)
                            else:
                                b = LEVELS[NL + 1 - v]
                                part = lambda t, z: t.rearrange("p (n z b) -> p n z b", z=2, b=b)[:, :, z, :]
                                ref = part(B, 0)[:, :, b - 1:b] if d == 0 else part(B, 1)[:, :, 0:1]
                                ref = ref.to_broadcast([P, TOK // (2 * b), b])
                                eng.tensor_tensor(part(F, 1 - d), part(B, 1 - d), ref, ALU.subtract).then_inc(dve.own, dve.step())
                                eng.tensor_tensor(part(F, d), ref, part(B, d), ALU.subtract).then_inc(dx_ready, 1)
                        if n >= 2:
                            h, v = divmod(n - 2, NL + 2)
                            src = bank[n % 2][:].rearrange("p (t n) -> p t n", t=TT)
                            dst = cAT[:, h, :].rearrange("p (t n) -> p t n", t=TT)
                            eng.wait_ge(lv_ready, dve.next(lv_ready))
                            if v == 0:
                                ins = eng.tensor_tensor(dst, src, ident.unsqueeze(1).to_broadcast([P, TT, P]), ALU.mult)
                            elif v == 1:
                                ins = eng.tensor_copy(ckl[:, h], src)
                            else:
                                lv = NL + 1 - v
                                eng.wait_ge(lv_used, dve.next(lv_used, 0))
                                m = msk[:, (NL if d else 0) + lv, :].unsqueeze(1).to_broadcast([P, TT, P])
                                ins = eng.copy_predicated(dst, m, src)
                            ins.then_inc(lv_used, 1)
                            dve.skip(lv_used)
                    eng.wait_ge(el_ready, dve.next(el_ready, C_HEADS))
                    for s in range(TT):
                        tl = s if d == 0 else s ^ 1
                        for hp in range(2):
                            dst = co[:, 4 * hp:4 * hp + 4, tl * P:(tl + 1) * P]
                            src = bank[4 + hp][:].rearrange("p (a b) -> p a b", a=4)
                            eng.wait_ge(od_ready, dve.next(od_ready))
                            if d == 0:
                                eng.tensor_copy(dst, src).then_inc(bo_ready, 1)
                            else:
                                eng.tensor_tensor(dst, dst, src, ALU.add).then_inc(bo_ready, 1)
                            eng.wait_ge(s_done, dve.next(s_done))
                            for j in range(2):
                                h = 2 * hp + j
                                ins = eng.scalar_tensor_tensor(cS[:, h, :], cS[:, h, :], cel[:, h, tl:tl + 1],
                                                               bank[6 + hp][:, j * C_VD:(j + 1) * C_VD], ALU.mult, ALU.add)
                            ins.then_inc(st_upd, 1)
                    dve.skip(st_upd, 2 * TT)
                    eng.wait_ge(st_upd, dve.next(st_upd, 0))
                eng.wait_ge(qf_ready, dve.next(qf_ready, 2))
                eng.wait_ge(kf_ready, dve.next(kf_ready, 2))
                eng.wait_ge(bo_ready, dve.next(bo_ready, 16))

            def head_finish(o, gate, heads, nw):
                for i in range(len(heads) + 1):
                    if i < len(heads):
                        r = sq[:, i % 2, :]
                        eng.wait_ge(rt_ready, dve.next(rt_ready))
                        eng.reciprocal(r, r).then_inc(dve.own, dve.step())
                        eng.wait_ge(dve.own, dve.count())
                        for m, t in enumerate(heads[i]):
                            ins = eng.scalar_tensor_tensor(o[:, t, :], o[:, t, :], vec[:, nw + m:nw + m + 1], r, ALU.mult, ALU.mult)
                            if m == len(heads[i]) - 1:
                                ins.then_inc(og_ready, 1)
                        eng.wait_ge(og_ready, dve.next(og_ready))
                        for m, t in enumerate(heads[i]):
                            eng.tensor_tensor(o[:, t, :], o[:, t, :], gate[:, t, :], ALU.mult).then_inc(og2_ready, 1)
                    if i >= 1:
                        for t in heads[i - 1]:
                            eng.wait_ge(oh_ready, dve.next(oh_ready))
                            eng.tensor_tensor(u_lo[:, t, :], o[:, t, :], u_hi[:, t, :].bitcast(F32), ALU.subtract).then_inc(o_ready, 1)

            def norm(l, w, final=False):
                S = toks(l)
                mean = bank[STAT[w][0]][:, S]
                eng.wait_ge(mean_ready, dve.next(mean_ready))
                for t in range(KT):
                    eng.tensor_tensor(x[:, t, S], x[:, t, S], mean, ALU.subtract).then_inc(c_ready, 1)
                eng.wait_ge(std_ready, dve.next(std_ready))
                eng.reciprocal(rstd[:, S], rstd[:, S]).then_inc(dve.own, dve.step())
                eng.wait_ge(dve.own, dve.count())
                for t in range(KT + 1):
                    if t < KT:
                        ins = eng.tensor_tensor(x[:, t, S], x[:, t, S], rstd[:, S], ALU.mult)
                        ins.then_inc(own["dve"] if final else xh_ready, 1)
                        if final:
                            dve.skip(own["dve"])
                    if t >= 1 and not final:
                        u_low(l, t - 1)

            eng.wait_ge(s_con, dve.next(s_con, 16 * 18))
            eng.tensor_copy(msk[:], msk_f[:]).then_inc(dve.own, dve.step())
            eng.tensor_scalar(nsink[:], sink[:], -1.0, None, ALU.mult).then_inc(dve.own, dve.step())
            eng.sem_inc(g_done, 2)
            for t in range(ROWT):
                eng.wait_ge(rows_t, dve.next(rows_t))
                eng.tensor_copy(vec[:, t * P:t * P + ROWS[t]], bank[t][:, 0:ROWS[t]]).then_inc(vec_ready, 1)
            for t in range(KT):
                eng.wait_ge(xt_done, dve.next(xt_done))
                eng.tensor_copy(x[:, t, :], bank[t][:]).then_inc(xt_copied, 1)
            eng.wait_ge(ada_done, dve.next(ada_done, ADA_FIRST))
            modulation(0, range(2))
            eng.wait_ge(xt_copied, dve.next(xt_copied, KT))
            for t in range(KT + 1):
                if t < KT:
                    eng.sem_inc(xh_ready, 1)
                if t >= 1:
                    u_low(0, t - 1)
            for l in range(LAYERS):
                T = toks(l)
                if KIND[l] == "attn":
                    attention(l)
                if l == 0:
                    eng.wait_ge(ada_done, dve.next(ada_done, 2))
                    modulation(0, range(2, 6))
                if KIND[l] == "gdn":
                    delta_net()
                    head_finish(bo, bg, [(h,) for h in range(B_HEADS)], GDNNW)
                if KIND[l] == "gla":
                    linear_attention()
                    head_finish(co, cg, [(2 * h, 2 * h + 1) for h in range(C_HEADS)], GLANW)
                if l > 0:
                    eng.wait_ge(x_ready, dve.next(x_ready, KT))
                for n in range(4):
                    eng.wait_ge(w_done, dve.next(w_done, 4))
                    for m in range(2):
                        residual(l, 0, 2 * n + m, (n % 2) * 2 + m)
                norm(l, 0)
                more = l + 1 < LAYERS

                per = {conv_c: 2, silu_done: 2, w_done: 8, own["dve"]: 2}
                if more:
                    eng.wait_ge(u_ready, KT * (2 * l + 2))
                    eng.sem_inc(gates["dve"], 1)
                    for n in range(2):
                        dve.skip(ada_loaded[n], 16)
                    per = {**per, own["dve"]: 2 + 4 * (KT - 1), ada_loaded[0]: 16, ada_loaded[1]: 16, ada_done: 2}
                with dve.loop(FT // 2, per) as i:
                    if more:
                        ada_products(0)
                    for m in range(2):
                        eng.wait_ge(conv_c, dve.next(conv_c))
                        dve.stand()
                        f = i * 2 + m
                        w0, w2 = (vec[:, bass.ds(f + CONVW(l, tap), 1)] for tap in (0, 2))
                        S = seqs(l)
                        v3 = lambda t, lo, hi: t.rearrange("p (s n) -> p s n", s=2)[:, S[0]:S[-1] + 1, lo:hi]
                        eng.scalar_tensor_tensor(v3(cv[:, m, :], 1, 256), v3(bank[m][:], 0, 255), w0,
                                                          v3(cv[:, m, :], 1, 256), ALU.mult, ALU.add).then_inc(dve.own, dve.step())
                        eng.wait_ge(dve.own, dve.count())
                        dve.stand()
                        eng.scalar_tensor_tensor(v3(cv[:, m, :], 0, 255), v3(bank[m][:], 1, 256), w2,
                                                 v3(cv[:, m, :], 0, 255), ALU.mult, ALU.add).then_inc(conv_done, 1)
                    if more:
                        ada_products(1)
                    eng.wait_ge(w_done, dve.next(w_done, 8))
                    dve.stand()
                    for m in range(2):
                        eng.wait_ge(silu_done, dve.next(silu_done))
                        dve.stand()
                        eng.tensor_tensor(g[:, bass.ds(i * 2 + m, 1), T].rearrange("p a n -> p (a n)"), cv[:, m, T],
                                          bank[2 + m][:, T], ALU.mult).then_inc(g_done, 1)
                if more:
                    eng.wait_ge(ada_done, dve.next(ada_done, 2))
                    modulation(l + 1)

                dve.skip(g_done, FT)
                eng.wait_ge(g_done, dve.next(g_done, 2))
                dve.skip(g_done, -2)

                def g_lo(slot, gf):
                    eng.wait_ge(gs_h, dve.next(gs_h))
                    dve.stand()
                    eng.tensor_tensor(gs_lo[:, slot, T], gf, gs_hi[:, slot, T].bitcast(F32), ALU.subtract).then_inc(gs_ready, 1)

                for f in range(4):
                    g_lo(f, g[:, f, T])
                with dve.loop(4, {gs_h: 4}) as i:
                    for j in range(4):
                        g_lo(j, g[:, bass.ds(i * 4 + 4 + j, 1), T].rearrange("p a n -> p (a n)"))
                for f in range(20, FT):
                    g_lo(f % 4, g[:, f, T])
                eng.wait_ge(x_ready, dve.next(x_ready, KT))
                eng.wait_ge(w_done, dve.next(w_done, 44))
                for t in range(KT):
                    residual(l, 1, t, t)
                norm(l, 1, final=(l == LAYERS - 1))
            S = slice(CTX, TOK)
            eng.wait_ge(dve.own, dve.count())
            l = LAYERS - 1
            for t in range(KT):
                eng.tensor_scalar(x[:, t, S], x[:, t, S], vec[:, LNG(l, 1, t):LNG(l, 1, t) + 1],
                                  vec[:, LNB(l, 1, t):LNB(l, 1, t) + 1], ALU.mult, ALU.add).then_inc(x_fin, 1)
            eng.wait_ge(xt_done, dve.next(xt_done))
            for j in range(2):
                eng.tensor_copy(xout[:, j, 0:512], bank[2 * j][:]).then_inc(dve.own, dve.step())
                eng.tensor_copy(xout[:, j, 512:1024], bank[2 * j + 1][:]).then_inc(x_out, 1)


INPUTS = ("x", "c", "ctx", "c_ctx", "ada_w", "ada_b", "ln_g", "ln_b", "ffn_w_up", "ffn_conv_w", "ffn_conv_b",
          "ffn_w_down", "attn_w_qkv", "attn_sink", "attn_w_o", "gdn_w_in", "gdn_conv_w", "gdn_a_log", "gdn_dt_bias",
          "gdn_norm_w", "gdn_w_o", "gla_w_in", "gla_w_gate2", "gla_gate_b", "gla_norm_w", "gla_w_o")


def kernel(**inputs):
    import concourse.bacc as bacc
    from concourse.bass_utils import run_bass_kernel_spmd

    nc = bacc.Bacc("TRN2", target_bir_lowering=False, num_devices=1)
    consts, masks = constants()
    arrays, aps = {}, {}
    for name in INPUTS + ("consts", "masks"):
        v = np.ascontiguousarray({"consts": consts, "masks": masks}.get(name) if name in ("consts", "masks") else inputs[name])
        arrays[f"in_{name}"] = v
        aps[name] = nc.dram_tensor(f"in_{name}", v.shape, mybir.dt.from_np(v.dtype), kind="ExternalInput").ap()
    out = nc.dram_tensor("out_x", (1, SEQ, D), F32, kind="ExternalOutput").ap()
    build(nc, aps, out)
    r = run_bass_kernel_spmd(nc, [arrays], core_ids=[0])
    return r.results[0]["out_x"]
```
